# Optimizing a Trainium2 kernel written in Bass

```python
import jax, jax.numpy as jnp
from jax import lax
import numpy as np

D_MODEL = 1024
BATCH = 1
SEQ = 2048
DEPTH = 1
DEC_BATCH = 8
DEC_SEQ = 1
PAST_LEN = 16384
PAGE_SIZE = 128

NH_M = 4
DHV = D_MODEL // NH_M
DQK = DHV // 2
D_M = NH_M * DHV
D_QK = NH_M * DQK
MLSTM_CHUNK = 64
F_BIAS_INIT = 3.0
D_C = D_MODEL
CONV_W = 3
EPS = 1e-6
NEG_BIG = -1e30

SPLIT_SIZES = (D_QK, D_QK, D_M, NH_M, NH_M, D_M, D_M, D_C, D_C, D_C, D_C, D_MODEL, D_MODEL)
N_IN = sum(SPLIT_SIZES)

kernel_name = "hybrid_mlstm_shortconv_gated_merge_step"

def rmsnorm(x, w):
    xf = x.astype(jnp.float32)
    xf = xf * lax.rsqrt(jnp.mean(xf * xf, axis=-1, keepdims=True) + EPS)
    return (xf * w.astype(jnp.float32)).astype(x.dtype)

def mlstm_chunkwise(q, k, v, ig, lf, C0, n0, m0):
    B, L = q.shape[0], q.shape[1]
    Lc = min(MLSTM_CHUNK, L)
    nc = -(-L // Lc)
    pad = nc * Lc - L
    if pad:
        pw = ((0, 0), (0, pad), (0, 0), (0, 0))
        q = jnp.pad(q, pw)
        k = jnp.pad(k, pw)
        v = jnp.pad(v, pw)
        lf = jnp.pad(lf, ((0, 0), (0, pad), (0, 0)))
        ig = jnp.pad(ig, ((0, 0), (0, pad), (0, 0)), constant_values=NEG_BIG)

    def to_chunks(a):
        a = a.reshape((B, nc, Lc) + a.shape[2:])
        return jnp.moveaxis(jnp.moveaxis(a, 1, 0), 3, 2)

    qs, ks, vs, igs, lfs = to_chunks(q), to_chunks(k), to_chunks(v), to_chunks(ig), to_chunks(lf)
    mask = jnp.tril(jnp.ones((Lc, Lc), dtype=bool))

    def step(carry, inp):
        C, n, m = carry
        qc, kc, vc, igc, lfc = inp
        b = jnp.cumsum(lfc, axis=-1)
        logD = b[..., :, None] - b[..., None, :] + igc[..., None, :]
        logD = jnp.where(mask, logD, NEG_BIG)
        inter = b + m[..., None]
        m_t = jnp.maximum(inter, jnp.max(logD, axis=-1))
        Dm = jnp.exp(logD - m_t[..., None])
        w_int = jnp.exp(inter - m_t)
        s = jnp.einsum('bhtd,bhsd->bhts', qc, kc) * Dm
        num = w_int[..., None] * jnp.einsum('bhvd,bhtd->bhtv', C, qc) + jnp.einsum('bhts,bhsv->bhtv', s, vc)
        den = w_int * jnp.einsum('bhd,bhtd->bht', n, qc) + jnp.sum(s, axis=-1)
        h = num / jnp.maximum(jnp.abs(den), jnp.exp(-m_t))[..., None]
        logw_end = b[..., -1:] - b + igc
        inter_end = b[..., -1] + m
        m_new = jnp.maximum(inter_end, jnp.max(logw_end, axis=-1))
        w_end = jnp.exp(logw_end - m_new[..., None])
        f_end = jnp.exp(inter_end - m_new)
        C_new = f_end[..., None, None] * C + jnp.einsum('bhs,bhsv,bhsd->bhvd', w_end, vc, kc)
        n_new = f_end[..., None] * n + jnp.einsum('bhs,bhsd->bhd', w_end, kc)
        return (C_new, n_new, m_new), h

    (C1, n1, m1), hs = lax.scan(step, (C0, n0, m0), (qs, ks, vs, igs, lfs))
    h = jnp.moveaxis(jnp.moveaxis(hs, 0, 1), 2, 3).reshape(B, nc * Lc, NH_M, DHV)[:, :L]
    return h, C1, n1, m1

def short_conv(u, conv0, w):
    L = u.shape[1]
    up = jnp.concatenate([conv0.astype(u.dtype), u], axis=1)
    y = w[0] * up[:, 0:L]
    for j in range(1, CONV_W):
        y = y + w[j] * up[:, j:j + L]
    return y, up[:, -(CONV_W - 1):]

def layer(x, C0, n0, m0, conv0, norm_w, w_in, b_i, b_f, head_norm_w, conv_w, w_proj_m, w_proj_c, w_out):
    B, L, _ = x.shape
    f32 = jnp.float32
    xn = rmsnorm(x, norm_w)
    proj = xn @ w_in
    offs = np.cumsum(SPLIT_SIZES)[:-1].tolist()
    q, k, v, i_pre, f_pre, o_pre, z_m, b_g, c_g, x_c, z_c, g_m, g_c = jnp.split(proj, offs, axis=-1)
    q = q.reshape(B, L, NH_M, DQK).astype(f32)
    k = k.reshape(B, L, NH_M, DQK).astype(f32) * (DQK ** -0.5)
    v = v.reshape(B, L, NH_M, DHV).astype(f32)
    ig = i_pre.astype(f32) + b_i.astype(f32)
    lf = jax.nn.log_sigmoid(f_pre.astype(f32) + b_f.astype(f32))
    h, C1, n1, m1 = mlstm_chunkwise(q, k, v, ig, lf, C0.astype(f32), n0.astype(f32), m0.astype(f32))
    h = h * lax.rsqrt(jnp.mean(h * h, axis=-1, keepdims=True) + EPS)
    h = (h.reshape(B, L, D_M) * head_norm_w.astype(f32)).astype(x.dtype)
    h = h * jax.nn.sigmoid(o_pre) * jax.nn.silu(z_m)
    y_m = h @ w_proj_m
    cv, conv1 = short_conv(c_g * x_c, conv0, conv_w)
    y_c = (jax.nn.silu(z_c) * b_g * cv) @ w_proj_c
    mix = jax.nn.sigmoid(g_m) * y_m + jax.nn.sigmoid(g_c) * y_c
    out = x + mix @ w_out
    return out, C1, n1, m1, conv1

def setup_inputs(seed: int = 0) -> dict:
    key = jax.random.key(seed)
    ks = jax.random.split(key, 17)
    nrm = jax.random.normal
    f32 = jnp.float32
    return {
        "x_prompt": nrm(ks[0], (BATCH, SEQ, D_MODEL), f32),
        "x_sample": nrm(ks[1], (DEC_BATCH, DEC_SEQ, D_MODEL), f32),
        "state_mlstm_C": 0.3 * nrm(ks[2], (DEPTH, DEC_BATCH, NH_M, DHV, DQK), f32),
        "state_mlstm_n": 0.3 * nrm(ks[3], (DEPTH, DEC_BATCH, NH_M, DQK), f32),
        "state_mlstm_m": 2.0 + nrm(ks[4], (DEPTH, DEC_BATCH, NH_M), f32),
        "state_conv": nrm(ks[5], (DEPTH, DEC_BATCH, CONV_W - 1, D_C), f32),
        "norm_w": 1.0 + 0.05 * nrm(ks[6], (DEPTH, D_MODEL), f32),
        "w_in": nrm(ks[7], (DEPTH, D_MODEL, N_IN), f32) * D_MODEL ** -0.5,
        "b_i": 0.1 * nrm(ks[8], (DEPTH, NH_M), f32),
        "b_f": F_BIAS_INIT + 0.5 * nrm(ks[9], (DEPTH, NH_M), f32),
        "head_norm_w": 1.0 + 0.05 * nrm(ks[10], (DEPTH, D_M), f32),
        "conv_w": nrm(ks[11], (DEPTH, CONV_W, D_C), f32) * CONV_W ** -0.5,
        "w_proj_m": nrm(ks[12], (DEPTH, D_M, D_MODEL), f32) * D_M ** -0.5,
        "w_proj_c": nrm(ks[13], (DEPTH, D_C, D_MODEL), f32) * D_C ** -0.5,
        "w_out": nrm(ks[14], (DEPTH, D_MODEL, D_MODEL), f32) * D_MODEL ** -0.5,
        "final_norm_w": 1.0 + 0.05 * nrm(ks[15], (D_MODEL,), f32),
    }

def reference(x_prompt, x_sample, state_mlstm_C, state_mlstm_n, state_mlstm_m, state_conv,
              norm_w, w_in, b_i, b_f, head_norm_w, conv_w, w_proj_m, w_proj_c, w_out, final_norm_w):
    f32 = jnp.float32
    bp = x_prompt.shape[0]
    xp, xs = x_prompt, x_sample
    Cp_l, np_l, mp_l, cp_l = [], [], [], []
    Cs_l, ns_l, ms_l, cs_l = [], [], [], []
    for l in range(DEPTH):
        w = (norm_w[l], w_in[l], b_i[l], b_f[l], head_norm_w[l], conv_w[l], w_proj_m[l], w_proj_c[l], w_out[l])
        C0 = jnp.zeros((bp, NH_M, DHV, DQK), f32)
        n0 = jnp.zeros((bp, NH_M, DQK), f32)
        m0 = jnp.zeros((bp, NH_M), f32)
        cv0 = jnp.zeros((bp, CONV_W - 1, D_C), xp.dtype)
        xp, Cp, npp, mp, cp = layer(xp, C0, n0, m0, cv0, *w)
        xs, Cs, ns, ms, cs = layer(xs, state_mlstm_C[l], state_mlstm_n[l], state_mlstm_m[l], state_conv[l], *w)
        Cp_l.append(Cp.astype(state_mlstm_C.dtype)); np_l.append(npp.astype(state_mlstm_n.dtype))
        mp_l.append(mp.astype(state_mlstm_m.dtype)); cp_l.append(cp.astype(state_conv.dtype))
        Cs_l.append(Cs.astype(state_mlstm_C.dtype)); ns_l.append(ns.astype(state_mlstm_n.dtype))
        ms_l.append(ms.astype(state_mlstm_m.dtype)); cs_l.append(cs.astype(state_conv.dtype))
    y_prompt = rmsnorm(xp, final_norm_w)
    y_sample = rmsnorm(xs, final_norm_w)
    new_C_prompt = jnp.stack(Cp_l)
    new_n_prompt = jnp.stack(np_l)
    new_m_prompt = jnp.stack(mp_l)
    new_conv_prompt = jnp.stack(cp_l)
    new_C_sample = jnp.stack(Cs_l)
    new_n_sample = jnp.stack(ns_l)
    new_m_sample = jnp.stack(ms_l)
    new_conv_sample = jnp.stack(cs_l)
    return (y_prompt, y_sample, new_C_prompt, new_n_prompt, new_m_prompt, new_conv_prompt,
            new_C_sample, new_n_sample, new_m_sample, new_conv_sample)


_drawn_inputs = setup_inputs


def setup_inputs(seed=0):
    import zlib

    import numpy as np

    out = dict(_drawn_inputs(seed))
    spreads = {}
    factors = {'head_norm_w': 6.729}
    for name, (base, spread) in spreads.items():
        noise = np.random.default_rng([zlib.crc32(name.encode()), seed]).standard_normal(out[name].shape)
        drawn = base * np.exp(spread * noise) if base else spread * noise
        out[name] = __import__('jax').numpy.asarray(drawn.astype(out[name].dtype))
    for name, factor in factors.items():
        out[name] = (out[name] * factor).astype(out[name].dtype)
    return out
```

```python
from contextlib import ExitStack

import numpy as np

import concourse.bass as bass
from concourse import mybir

F32 = mybir.dt.float32
F32R = mybir.dt.float32r
ALU = mybir.AluOpType
ACT = mybir.ActivationFunctionType
AX = mybir.AxisListType

P = 128
D = 1024
KB = D // P
L = 2048
NS = 8
T = L + NS
NH, DQK, DHV = 4, 128, 256
NCH = L // P
HC = NCH * NH
CW = 3
EPS = 1e-6
NEG = -1e30
BIG = 3e38
COL = dict(q=0, k=512, v=1024, o=2056, z=3080, b=4104, c=5128, x=6152, s=7176, gm=8200, gc=9224)
VW = D + 2 * NH
VC = VW // 3
NT = L // P + 1
TILES = [(0, 412), (412, 412), (824, 412), (1236, 410), (1646, 410)]
NTILE = len(TILES)
TN = 294
NTC = 7
TP = TN * NTC
QSCALE = DQK ** -0.5


class Chain:

    def __init__(self, eng, sem):
        self.eng, self.sem, self.base, self.n = eng, sem, 0, 0

    def link(self, ins):
        ins.then_inc(self.sem, 1)
        self.n += 1
        self.eng.wait_ge(self.sem, self.base + self.n)

    def enter(self, i, per):
        self.saved, self.per = self.base + self.n, per
        self.base, self.n = self.saved + i * per, 0

    def leave(self, rounds):
        assert self.n == self.per, (self.n, self.per)
        self.base, self.n = self.saved + rounds * self.per, 0


def sbuf(nc, ctx, name, shape, dt=F32):
    return ctx.enter_context(nc.sbuf_tensor(name, shape, dt))


def psum(nc, ctx, name, shape):
    return ctx.enter_context(nc.psum_tensor(name, shape, F32))


class Shared:
    pass


def build(nc, inputs, outputs):
    def dram(name, *shape):
        return nc.dram_tensor(name, shape, F32, kind="Internal").ap()

    top, early = ExitStack(), ExitStack()
    with top:
        top.enter_context(nc.allow_non_contiguous_dma(reason="small per-channel columns"))
        RH = sbuf(nc, top, "RH", [P, KB, T], F32R)
        RL = sbuf(nc, top, "RL", [P, KB, T], F32R)
        g = Shared()
        (g.x_prompt, g.x_sample, g.state_C, g.state_n, g.state_m, g.state_conv, g.norm_w, g.w_in, g.b_i, g.b_f,
         g.head_norm_w, g.conv_w, g.w_proj_m, g.w_proj_c, g.w_out, g.final_norm_w) = inputs
        (g.y_prompt, g.y_sample, g.C_prompt, g.n_prompt, g.m_prompt, g.conv_prompt,
         g.C_sample, g.n_sample, g.m_sample, g.conv_sample) = outputs
        g.v_rows = dram("v_rows", T, D)
        g.qT_d = dram("qT_d", NH, P, TP)
        g.kT_d = dram("kT_d", NH, P, TP)
        g.gate_d = dram("gate_d", KB, P, TP)
        g.hg_d = dram("hg_d", KB, P, TP)
        g.cv_d = dram("cv_d", KB, P, TP)
        g.tm_d = dram("tm_d", KB, P, TP)
        g.tc_d = dram("tc_d", KB, P, TP)
        g.mix_d = dram("mix_d", KB, P, TP)
        g.negM_d = dram("negM_d", NCH, NH, P)
        g.qk_rows = dram("qk_rows", NS, 2 * NH * DQK)
        g.fir_d = dram("fir_d", 3, NS * NH)
        g.RH, g.RL, g.RHf = RH, RL, RH[:, :, :].bitcast(F32)
        g.ident = sbuf(nc, top, "ident", [P, P])
        g.IF = sbuf(nc, early, "IF", [P, NT, 2 * NH])
        with early:
            phase_a(nc, g)
            phase_b(nc, g)
        phase_c(nc, g)
        phase_d(nc, g)


def phase_a(nc, g):
    ctx = ExitStack()
    sem = lambda n: ctx.enter_context(nc.semaphore("a_" + n))
    WH = sbuf(nc, ctx, "wv_hi", [P, KB, VW], F32R)
    WL = sbuf(nc, ctx, "wv_lo", [P, KB, VW], F32R)
    xt = [sbuf(nc, ctx, f"xt{j}", [P, D]) for j in range(2)]
    stage = [sbuf(nc, ctx, f"wv_stage{j}", [P, VW]) for j in range(2)]
    v_out, junk = stage[0], stage[1]
    nw = sbuf(nc, ctx, "nw", [P, D])
    stat = sbuf(nc, ctx, "stat", [P, 3, 2])
    half = sbuf(nc, ctx, "half", [P, 1])
    TR = [psum(nc, ctx, f"a_tr{j}", [P, 4, P]) for j in range(2)]
    V = [psum(nc, ctx, f"a_v{j}", [P, 512]) for j in range(6)]

    x_in = [sem("x_in0"), sem("x_in1")]
    wv_in = [sem("wv_in0"), sem("wv_in1")]
    const_in, const_set = sem("const_in"), sem("const_set")
    wv_hi, wv_lo = sem("wv_hi"), sem("wv_lo")
    squared, var_set, rstd_set, normed = sem("squared"), sem("var_set"), sem("rstd_set"), sem("normed")
    transposed, hi_set, lo_set = sem("transposed"), sem("hi_set"), sem("lo_set")
    v_done, v_act, v_dve, v_stored = sem("v_done"), sem("v_act"), sem("v_dve"), sem("v_stored")
    if_set = sem("if_set")

    def rows(i):
        return NS if isinstance(i, int) and i == NT - 1 else P

    xp = g.x_prompt[0].rearrange("(t p) d -> t p d", p=P)
    w_v = g.w_in[0].rearrange("(k p) n -> k p n", p=P)

    def over_tiles(eng, first, body):
        first()
        with eng.Fori(0, 7) as j:
            body(2 * j + 1, 1)
            body(2 * j + 2, 0)
        body(NT - 2, 1)
        body(NT - 1, 0)

    with nc.Block() as block:

        @block.sync
        def _(sp):
            sp.dma_start(xt[0][:, :], xp[0]).then_inc(x_in[0], 16)
            sp.dma_start(nw[:, :], g.norm_w[0].partition_broadcast(P)).then_inc(const_in, 16)
            for k in range(KB):
                if k >= 2:
                    sp.wait_ge(wv_lo, k - 1)
                sp.dma_start(stage[k % 2][:, :], w_v[k, :, COL["v"]:COL["v"] + VW]).then_inc(wv_in[k % 2], 16)
                if k == 0:
                    sp.dma_start(xt[1][:, :], xp[1]).then_inc(x_in[1], 16)

            def load_and_store(i, par):
                if not isinstance(i, int):
                    sp.wait_ge(transposed, i)
                    sp.dma_start(xt[1 - par][:, :], xp[bass.ds(i + 1, 1)].rearrange("a p d -> (a p) d")).then_inc(x_in[1 - par], 16)
                elif i == NT - 2:
                    sp.wait_ge(transposed, i)
                    sp.dma_start(xt[1 - par][:NS, :], g.x_sample[:, 0, :]).then_inc(x_in[1 - par], 16)
                store(i - 1, P)

            def store(i, n):
                sp.wait_ge(v_act, i + 1)
                sp.wait_ge(v_dve, i + 1)
                dst = g.v_rows[i * P:i * P + n, :] if isinstance(i, int) else g.v_rows[bass.ds(i * P, n), :]
                sp.dma_start(dst, v_out[:n, 0:D]).then_inc(v_stored, 16)

            over_tiles(sp, lambda: None, load_and_store)
            store(NT - 1, NS)
            sp.wait_ge(v_stored, 16 * NT)

        @block.gpsimd
        def _(pool):
            nc.gpsimd.memset(half[:, :], -0.5).then_inc(const_set, 1)
            nc.gpsimd.memset(g.ident[:, :], 0.0).then_inc(const_set, 1)
            pool.wait_ge(const_set, 2)
            nc.gpsimd.affine_select(out=g.ident[:, :], in_=g.ident[:, :], compare_op=ALU.not_equal, fill=1.0,
                                    base=0, pattern=[[-1, P]], channel_multiplier=1).then_inc(const_set, 1)

            def rstd(i, par):
                n = rows(i)
                pool.wait_ge(var_set, i + 1)
                nc.gpsimd.tensor_tensor(stat[:n, 2, par:par + 1], stat[:n, 1, par:par + 1], half[:n, :],
                                        ALU.pow).then_inc(rstd_set, 1)

            over_tiles(pool, lambda: rstd(0, 0), rstd)

        @block.scalar
        def _(act):
            def square(i, par):
                n = rows(i)
                act.wait_ge(x_in[par], 8 * i + (8 if par else 16))
                act.wait_ge(wv_lo, KB)
                nc.scalar.activation(junk[:n, 0:D], xt[par][:n, :], ACT.Square,
                                     accum_out=stat[:n, 0, par:par + 1]).then_inc(squared, 1)

            def hi(i):
                n = rows(i)
                act.wait_ge(transposed, i + 1)
                for j in range(2):
                    dst = g.RH[:, 4 * j:4 * j + 4, i * P:i * P + n] if isinstance(i, int) else g.RH[:, 4 * j:4 * j + 4, bass.ds(i * P, n)]
                    nc.scalar.activation(dst, TR[j][:, :, 0:n], ACT.Copy).then_inc(hi_set, 1)

            def evac(i, par):
                n = rows(i)
                act.wait_ge(v_done, i + 1)
                act.wait_ge(v_stored, 16 * i)
                nc.scalar.activation(v_out[:n, VC:2 * VC], V[3 * par + 1][:n, 0:VC], ACT.Copy).then_inc(v_act, 1)

            def first():
                for k in range(KB):
                    act.wait_ge(wv_in[k % 2], 16 * (k // 2 + 1))
                    nc.scalar.activation(WH[:, k, :], stage[k % 2][:, :], ACT.Copy).then_inc(wv_hi, 1)
                square(0, 0)
                hi(0)

            def body(i, par):
                square(i, par)
                hi(i)
                evac(i - 1, 1 - par)

            over_tiles(act, first, body)
            evac(NT - 1, 0)

        @block.vector
        def _(dve):
            def norm(i, par):
                n = rows(i)
                dve.wait_ge(squared, i + 1)
                nc.vector.tensor_scalar(stat[:n, 1, par:par + 1], stat[:n, 0, par:par + 1], 1.0 / D, EPS,
                                        ALU.mult, ALU.add).then_inc(var_set, 1)
                dve.wait_ge(rstd_set, i + 1)
                nc.vector.scalar_tensor_tensor(out=xt[par][:n, :], in0=xt[par][:n, :], scalar=stat[:n, 2, par:par + 1],
                                               in1=nw[:n, :], op0=ALU.mult, op1=ALU.mult).then_inc(normed, 1)

            def lo(i):
                n = rows(i)
                for j in range(2):
                    dve.wait_ge(hi_set, 2 * i + j + 1)
                    at = slice(i * P, i * P + n) if isinstance(i, int) else bass.ds(i * P, n)
                    nc.vector.tensor_tensor(g.RL[:, 4 * j:4 * j + 4, at], TR[j][:, :, 0:n],
                                            g.RHf[:, 4 * j:4 * j + 4, at], ALU.subtract).then_inc(lo_set, 1)

            def evac(i, par):
                n = rows(i)
                dve.wait_ge(v_done, i + 1)
                dve.wait_ge(v_stored, 16 * i)
                nc.vector.tensor_copy(v_out[:n, 0:VC], V[3 * par][:n, 0:VC])
                gates = g.IF[:n, i, :] if isinstance(i, int) else g.IF[:n, bass.ds(i, 1), :].rearrange("p a n -> p (a n)")
                nc.vector.tensor_copy(gates, V[3 * par + 2][:n, D - 2 * VC:VC])
                nc.vector.tensor_copy(v_out[:n, 2 * VC:D], V[3 * par + 2][:n, 0:D - 2 * VC]).then_inc(v_dve, 1)

            def first():
                for k in range(KB):
                    dve.wait_ge(wv_hi, k + 1)
                    nc.vector.tensor_tensor(WL[:, k, :], stage[k % 2][:, :], WH[:, k, :].bitcast(F32),
                                            ALU.subtract).then_inc(wv_lo, 1)
                dve.wait_ge(const_in, 16)
                norm(0, 0)
                lo(0)

            def body(i, par):
                norm(i, par)
                lo(i)
                evac(i - 1, 1 - par)

            over_tiles(dve, first, body)
            evac(NT - 1, 0)

        @block.tensor
        def _(pe):
            def transpose(i):
                n = rows(i)
                pe.wait_ge(normed, i + 1)
                if i:
                    pe.wait_ge(lo_set, 2 * i)
                for k in range(KB):
                    last = nc.tensor.transpose(TR[k // 4][:, k % 4, 0:n], xt[i % 2][:n, k * P:(k + 1) * P],
                                               g.ident[:n, :n])
                last.then_inc(transposed, 1)

            def project(i):
                n = rows(i)
                pe.wait_ge(lo_set, 2 * i + 2)
                if i >= 2:
                    pe.wait_ge(v_act, i - 1)
                    pe.wait_ge(v_dve, i - 1)
                for j in range(3):
                    step = 0
                    for k in range(KB):
                        for x, w in ((g.RH, WH), (g.RH, WL), (g.RL, WH)):
                            last = nc.tensor.matmul(V[3 * (i % 2) + j][:n, 0:VC], x[:, k, i * P:i * P + n],
                                                    w[:, k, j * VC:(j + 1) * VC], start=(step == 0), stop=(step == 3 * KB - 1))
                            step += 1
                last.then_inc(v_done, 1)

            pe.wait_ge(const_set, 3)
            transpose(0)
            pe.wait_ge(wv_lo, KB)
            for i in range(NT):
                if i + 1 < NT:
                    transpose(i + 1)
                project(i)

    ctx.close()


def phase_b(nc, g):
    ctx = ExitStack()
    sem = lambda n: ctx.enter_context(nc.semaphore("b_" + n))
    WS = sbuf(nc, ctx, "w_stage", [P, 2, KB, P])
    WH = sbuf(nc, ctx, "w_hi", [P, 2, KB, P], F32R)
    WL = sbuf(nc, ctx, "w_lo", [P, 2, KB, P], F32R)
    E0 = sbuf(nc, ctx, "row0", [P, TP])
    E1 = sbuf(nc, ctx, "row1", [P, TP])
    ZT = sbuf(nc, ctx, "z_tanh", [P, 2, 412])
    CV = sbuf(nc, ctx, "conv_tile", [P, 412])
    kT = sbuf(nc, ctx, "kT", [P, NH, P])
    qT = sbuf(nc, ctx, "qT", [P, NH, P])
    va = sbuf(nc, ctx, "v_ones", [P, NH, DHV + 1])
    nM = sbuf(nc, ctx, "negM", [P, NH, P])
    Dm = sbuf(nc, ctx, "decay", [P, NH, P])
    QW = sbuf(nc, ctx, "q_weighted", [P, NH, P])
    PT_ = sbuf(nc, ctx, "scores", [P, NH, P])
    KW = sbuf(nc, ctx, "k_weighted", [P, NH, P])
    HB = sbuf(nc, ctx, "h", [P, NH, DHV])
    GT = sbuf(nc, ctx, "gate", [P, KB, P])
    CS = sbuf(nc, ctx, "C_state", [P, NH, DHV + 1])
    mask = sbuf(nc, ctx, "mask", [P, P])
    cumU = sbuf(nc, ctx, "cum_upper", [P, P])
    ones = sbuf(nc, ctx, "ones", [P, P])
    half = sbuf(nc, ctx, "minus_half", [P, HC])
    bif = sbuf(nc, ctx, "b_if", [P, 2 * NH])
    hnw = sbuf(nc, ctx, "head_norm_q", [P, KB])
    cw = sbuf(nc, ctx, "conv_w_half", [P, CW, KB])
    cs = sbuf(nc, ctx, "conv_state", [P, KB, 2 * NS])
    csr = PT_[:2 * NS, :, :].rearrange("p a b -> p (a b)")
    csr2 = KW[:2 * NS, :, :].rearrange("p a b -> p (a b)")
    names = ("f_log", "f_abs", "b_cum", "a_in", "exp_negm", "w_end", "f_end", "m_prev")
    tk = {n: sbuf(nc, ctx, n, [P, HC]) for n in names}
    aT = GT[:HC, 0, :]
    cM = GT[:HC, 1, :]
    rowA = sbuf(nc, ctx, "row_A", [1, 4, HC + NH])
    col = sbuf(nc, ctx, "m_prev_col", [HC, 1])
    ss = sbuf(nc, ctx, "sumsq", [P, 3, NH])
    den = sbuf(nc, ctx, "den", [P, 2, 2])
    sm = sbuf(nc, ctx, "sample_small", [NS, 12, NH])
    dec = sbuf(nc, ctx, "sample_wide", [P, 8, 2 * NS * NH])
    G = [psum(nc, ctx, f"b_g{j}", [P, 512]) for j in range(2)]
    PS = psum(nc, ctx, "b_s", [P, NH, P])
    PT = [psum(nc, ctx, f"b_t{j}", [P, NH, P]) for j in range(2)]
    PN = [psum(nc, ctx, f"b_n{j}", [P, 512]) for j in range(2)]
    PC = psum(nc, ctx, "b_c", [P, 512])

    w_in_v = g.w_in[0].rearrange("(k p) n -> p k n", p=P)

    w_in_s = [sem("w_in0"), sem("w_in1")]
    w_hi, w_ready = sem("w_hi"), sem("w_ready")
    done = sem("tile_done")
    free = [sem("bank_free0"), sem("bank_free1")]
    z_set = sem("z_set")
    gate_set, u_used = sem("gate_set"), sem("u_used")
    row_out = [sem("row_out0"), sem("row_out1")]
    conv_out, state_out, misc_out = sem("conv_out"), sem("state_out"), sem("misc_out")
    const_in, const_set, pads = sem("const_in"), sem("const_set"), sem("pads")
    kq_in, v_in, gate_in, hg_out = sem("kq_in"), sem("v_in"), sem("gate_in"), sem("hg_out")
    s_done, kt_done, num_done, cu_done, ht_done = (sem(n) for n in ("s_done", "kt_done", "num_done", "cu_done", "ht_done"))
    dpre, kw_set, qw_set, p_set = sem("dpre"), sem("kw_set"), sem("qw_set"), sem("p_set")
    wint_set, dexp_set, sq_set = sem("wint_set"), sem("dexp_set"), sem("sq_set")
    h_set, c_set, var_set, rs_set, hn_set, hg_set = (sem(n) for n in ("h_set", "c_set", "var_set", "rs_set", "hn_set", "hg_set"))
    biased, act_own, softplus, lf_set, b_mm, a_set, a_mm, cm_set, al_mm, m_set, m_mm, M_set, mt_mm, exps_in, exps_set = (
        sem(n) for n in ("biased", "act_own", "softplus", "lf_set", "b_mm", "a_set", "a_mm", "cm_set", "al_mm", "m_set",
                         "m_mm", "M_set", "mt_mm", "exps_in", "exps_set"))
    dve_own = sem("dve_own")
    ct_mm, ct_set, c_out = sem("ct_mm"), sem("ct_set"), sem("c_out")
    dec_in, dec_mm, dec_rows, dec_out, dec_bc = (sem(n) for n in ("dec_in", "dec_mm", "dec_rows", "dec_out", "dec_bc"))
    dec_kq_in, dec_c_in, dec_upd = sem("dec_kq_in"), sem("dec_c_in"), sem("dec_upd")
    dec_sq, dec_sum, dec_var, dec_rs, dec_h = (sem(n) for n in ("dec_sq", "dec_sum", "dec_var", "dec_rs", "dec_h"))

    def sl(i, n=1):
        return slice(i * n, i * n + n) if isinstance(i, int) else bass.ds(i * n, n)

    NP1, NP2, NP3, NP4 = 4, 8, 16, 8
    F1, F2, F3, F4 = 0, NP1, NP1 + NP2, NP1 + NP2 + NP3
    NPAIR = F4 + NP4

    def block_waits(eng, pair, par):
        eng.wait_ge(free[par], NTILE * pair + (NTILE if par else 3) + 1)

    def bc(ap, n):
        return ap.unsqueeze(2).to_broadcast([ap.shape[0], ap.shape[1], n])

    row_q, row_k, row_gate, row_conv, row_tm, row_tc = 0, 0, NP1, NP1 + NP2, NP1, NP1 + NP2 + KB

    with nc.Block() as block:

        @block.sync
        def _(sp):
            def load_w(m_par, pair, c0):
                if not (isinstance(pair, int) and pair == 0):
                    sp.wait_ge(w_ready, 2 * pair + m_par - 1)
                sp.dma_start(WS[:, m_par], w_in_v[:, :, bass.ds(c0, P)]).then_inc(w_in_s[m_par], 16)

            load_w(0, 0, COL["q"])
            load_w(1, 0, COL["k"])
            sp.dma_start(bif[:, 0:NH], g.b_i[0].partition_broadcast(P)).then_inc(const_in, 16)
            sp.dma_start(bif[:, NH:], g.b_f[0].partition_broadcast(P)).then_inc(const_in, 16)
            sp.dma_start(hnw[:, :], g.head_norm_w[0].rearrange("(k p) -> p k", p=P)).then_inc(const_in, 16)
            for j in range(CW):
                sp.dma_start(cw[:, j, :], g.conv_w[0, j].rearrange("(k p) -> p k", p=P)).then_inc(const_in, 16)
            state = g.state_conv[0].rearrange("b r d -> (b r) d")
            sp.dma_start(csr, state[:, 0:512]).then_inc(const_in, 16)
            sp.dma_start(csr2, state[:, 512:D]).then_inc(const_in, 16)
            sp.dma_start(sm[:, 0, :], g.state_m[0]).then_inc(const_in, 16)
            sp.dma_start(g.conv_sample[0, :, 0, :], g.state_conv[0, :, 1, :]).then_inc(state_out, 16)
            sp.wait_ge(const_set, 1)
            for a in (g.hg_d, g.cv_d, g.tm_d, g.tc_d):
                sp.dma_start(a[:, :, T:TP].rearrange("k p n -> p k n"),
                             dec[:, 0, 0:2 * KB].rearrange("p (k n) -> p k n", k=KB)).then_inc(pads, 16)
            sp.wait_ge(M_set, 1)
            sp.dma_start(g.negM_d.rearrange("c h t -> (c h) t"), aT).then_inc(misc_out, 16)
            sp.dma_start(g.m_prompt[0], rowA[0:1, 2, HC:HC + NH]).then_inc(misc_out, 16)
            sp.dma_start(g.m_sample[0], sm[:, 3, :]).then_inc(misc_out, 16)

            def one(a, i):
                return a[i] if isinstance(i, int) else a[bass.ds(i, 1)].rearrange("a p n -> (a p) n")

            def qk(h, last=False):
                pair = F1 + h
                load_w(0, pair + 1, COL["o"] if last else COL["q"] + (h + 1) * P)
                load_w(1, pair + 1, COL["z"] if last else COL["k"] + (h + 1) * P)
                block_waits(sp, pair, 0)
                sp.dma_start(one(g.qT_d, h)[:, 0:T], E0[:, 0:T]).then_inc(row_out[0], 16)
                block_waits(sp, pair, 1)
                sp.dma_start(one(g.kT_d, h)[:, 0:T], E1[:, 0:T]).then_inc(row_out[1], 16)

            with sp.Fori(0, NP1 - 1) as h:
                qk(h)
            qk(NP1 - 1, True)

            def oz(i, last=False):
                pair = F2 + i
                load_w(0, pair + 1, COL["c"] if last else COL["o"] + (i + 1) * P)
                load_w(1, pair + 1, COL["x"] if last else COL["z"] + (i + 1) * P)
                sp.wait_ge(gate_set, i + 1)
                sp.dma_start(one(g.gate_d, i)[:, 0:T], E1[:, 0:T]).then_inc(row_out[1], 16)

            with sp.Fori(0, NP2 - 1) as i:
                oz(i)
            oz(NP2 - 1, True)

            def load_kq(c):
                if not (isinstance(c, int) and c == 0):
                    sp.wait_ge(p_set, c)
                at = sl(c, P)
                sp.dma_start(kT[:, :, :], g.kT_d[:, :, at].rearrange("h p t -> p h t")).then_inc(kq_in, 16)
                sp.dma_start(qT[:, :, :], g.qT_d[:, :, at].rearrange("h p t -> p h t")).then_inc(kq_in, 16)
                sp.dma_start(nM[:, :, :], (g.negM_d[c] if isinstance(c, int) else g.negM_d[bass.ds(c, 1)].rearrange("a h t -> (a h) t")).partition_broadcast(P)).then_inc(kq_in, 16)

            def load_v(c):
                if not (isinstance(c, int) and c == 0):
                    sp.wait_ge(cu_done, NH * c)
                sp.dma_start(va[:, :, 0:DHV], g.v_rows[sl(c, P), :].rearrange("t (h v) -> t h v", h=NH)).then_inc(v_in, 16)

            def load_gate(c):
                sp.wait_ge(hg_out, 16 * c)
                sp.dma_start(GT[:, :, :], g.gate_d[:, :, sl(c, P)].rearrange("k p t -> p k t")).then_inc(gate_in, 16)

            def store_hg(c):
                sp.wait_ge(hg_set, c + 1)
                sp.dma_start(g.hg_d[:, :, sl(c, P)].rearrange("k p t -> p k t"), GT[:, :, :]).then_inc(hg_out, 16)

            sp.wait_ge(row_out[0], 16 * NP1)
            sp.wait_ge(row_out[1], 16 * (NP1 + NP2))
            sp.wait_ge(misc_out, 48)
            load_kq(0)
            load_v(0)
            load_gate(0)

            def conv(i, last=False):
                pair = F3 + 2 * i
                c = 2 * i
                load_w(0, pair + 1, COL["s"] + i * P)
                load_kq(c + 1)
                load_w(1, pair + 1, COL["b"] + i * P)
                load_v(c + 1)
                store_hg(c)
                load_gate(c + 1)
                block_waits(sp, pair, 1)
                sp.dma_start(g.conv_sample[0, :, 1, sl(i, P)].rearrange("b d -> d b"), E0[:, L + 2:L + 2 + NS]).then_inc(conv_out, 16)
                sp.dma_start(g.conv_prompt[0, 0][:, sl(i, P)].rearrange("r d -> d r"), E0[:, L:L + 2]).then_inc(conv_out, 16)
                load_w(0, pair + 2, COL["gm"] if last else COL["c"] + (i + 1) * P)
                if not last:
                    load_kq(c + 2)
                load_w(1, pair + 2, COL["gc"] if last else COL["x"] + (i + 1) * P)
                if not last:
                    load_v(c + 2)
                store_hg(c + 1)
                if not last:
                    load_gate(c + 2)
                block_waits(sp, pair + 1, 1)
                sp.dma_start(one(g.cv_d, i)[:, 0:T], E1[:, 0:T]).then_inc(row_out[1], 16)

            with sp.Fori(0, KB - 1) as i:
                conv(i)
            conv(KB - 1, True)

            sp.wait_ge(hg_out, 16 * NCH)
            sp.dma_start(GT[:, 0, 0:NH * NS].rearrange("p (h b) -> p h b", h=NH),
                         g.qT_d[:, :, L:T].rearrange("h p b -> p h b")).then_inc(dec_in, 16)
            sp.dma_start(GT[:, 0, NH * NS:2 * NH * NS].rearrange("p (h b) -> p h b", h=NH),
                         g.kT_d[:, :, L:T].rearrange("h p b -> p h b")).then_inc(dec_in, 16)
            sp.dma_start(dec[:, 7, :].rearrange("p (k b) -> p k b", k=KB),
                         g.gate_d[:, :, L:T].rearrange("k p b -> p k b")).then_inc(dec_in, 16)
            sp.dma_start(QW[:NS, :, :], g.state_n[0]).then_inc(dec_in, 16)
            sp.dma_start(va[:NS, 0:NH, 0:DHV], g.v_rows[L:T, :].rearrange("t (h v) -> t h v", h=NH)).then_inc(dec_in, 16)
            load_w(0, F4 + 1, COL["gm"] + P)
            load_w(1, F4 + 1, COL["gc"] + P)
            sp.wait_ge(ct_set, 1)
            for h in range(NH):
                sp.dma_start(g.C_prompt[0, 0, h].rearrange("(a v) d -> v a d", v=P), HB[:, h, :].rearrange("p (a d) -> p a d", a=2)).then_inc(c_out, 16)
            sp.dma_start(g.n_prompt[0, 0].rearrange("h d -> d h"), CS[:, :, DHV]).then_inc(c_out, 16)
            sp.wait_ge(dec_rows, 1)
            sp.dma_start(g.qk_rows[:, 0:512], PT_[:NS, :, :].rearrange("p h d -> p (h d)")).then_inc(dec_out, 16)
            sp.dma_start(g.qk_rows[:, 512:1024], KW[:NS, :, :].rearrange("p h d -> p (h d)")).then_inc(dec_out, 16)
            sp.dma_start(g.n_sample[0], QW[:NS, :, :]).then_inc(dec_out, 16)
            for j in range(3):
                sp.dma_start(g.fir_d[j].rearrange("(b h) -> b h", h=NH), sm[:, 5 + j, :]).then_inc(dec_out, 16)
            sp.wait_ge(dec_out, 16 * 6)
            sp.wait_ge(pads, 64)
            sp.dma_start(dec[:, 0, :], g.fir_d[0:2].rearrange("j n -> (j n)").partition_broadcast(P)).then_inc(dec_bc, 16)
            sp.dma_start(dec[:, 1, 0:NS * NH], g.fir_d[2].partition_broadcast(P)).then_inc(dec_bc, 16)

            def load_sample(b):
                rows = g.qk_rows[b] if isinstance(b, int) else g.qk_rows[bass.ds(b, 1)].rearrange("a n -> (a n)")
                sp.wait_ge(dec_upd, b)
                sp.dma_start(qT[:, :, :].rearrange("p h d -> p (h d)"), rows[0:512].partition_broadcast(P)).then_inc(dec_kq_in, 16)
                sp.dma_start(kT[:, :, :].rearrange("p h d -> p (h d)"), rows[512:1024].partition_broadcast(P)).then_inc(dec_kq_in, 16)
                sp.wait_ge(state_out, 16 * (b + 1))
                src = g.state_C[0, b] if isinstance(b, int) else g.state_C[0, bass.ds(b, 1)].rearrange("a h v d -> (a h) v d")
                sp.dma_start(GT[:, :, :], src.rearrange("h (a v) d -> v (h a) d", v=P)).then_inc(dec_c_in, 16)

            def gates(i, last=False):
                pair = F4 + i
                load_sample(i)
                block_waits(sp, pair, 0)
                sp.dma_start(one(g.tm_d, i)[:, 0:T], E0[:, 0:T]).then_inc(row_out[0], 16)
                block_waits(sp, pair, 1)
                sp.dma_start(one(g.tc_d, i)[:, 0:T], E1[:, 0:T]).then_inc(row_out[1], 16)
                if not last:
                    load_w(0, pair + 2, COL["gm"] + (i + 2) * P)
                    load_w(1, pair + 2, COL["gc"] + (i + 2) * P)
                sp.wait_ge(dec_upd, i + 1)
                dst = g.C_sample[0, i] if isinstance(i, int) else g.C_sample[0, bass.ds(i, 1)].rearrange("a h v d -> (a h) v d")
                sp.dma_start(dst.rearrange("h (a v) d -> v (h a) d", v=P), GT[:, :, :]).then_inc(state_out, 16)

            with sp.Fori(0, NP4 - 2) as i:
                gates(i)
            gates(NP4 - 2, True)
            gates(NP4 - 1, True)
            sp.wait_ge(dec_h, 1)
            sp.dma_start(g.hg_d[:, :, L:T].rearrange("k p b -> p k b"),
                         dec[:, 6, :].rearrange("p (k b) -> p k b", k=KB)).then_inc(hg_out, 16)
            for s, v in ((row_out[0], 16 * (NP1 + NP4)), (row_out[1], 16 * (NP1 + NP2 + KB + NP4)), (hg_out, 16 * (NCH + 1)),
                         (pads, 64), (c_out, 16 * 5), (state_out, 16 * 9), (conv_out, 32 * KB), (misc_out, 48), (dec_out, 96)):
                sp.wait_ge(s, v)

        @block.gpsimd
        def _(pool):
            nc.gpsimd.memset(dec[:, 0, 0:2 * KB], 0.0).then_inc(const_set, 1)
            nc.gpsimd.memset(half[:, :], -0.5)
            nc.gpsimd.memset(ones[:, :], 1.0).then_inc(const_set, 1)
            nc.gpsimd.memset(mask[:, :], BIG).then_inc(const_set, 1)
            nc.gpsimd.memset(va[:, :, DHV], 1.0).then_inc(const_set, 1)
            pool.wait_ge(const_set, 3)
            nc.gpsimd.affine_select(out=cumU[:, :], in_=ones[:, :], compare_op=ALU.is_ge, fill=0.0,
                                    base=0, pattern=[[1, P]], channel_multiplier=-1).then_inc(const_set, 1)
            nc.gpsimd.affine_select(out=mask[:, :], in_=mask[:, :], compare_op=ALU.is_ge, fill=NEG,
                                    base=0, pattern=[[1, P]], channel_multiplier=-1).then_inc(const_set, 1)
            with pool.Fori(0, NCH) as c:
                pool.wait_ge(var_set, c + 1)
                nc.gpsimd.tensor_tensor(ss[:, 2, :], ss[:, 1, :], half[:, 0:NH], ALU.pow).then_inc(rs_set, 1)
            pool.wait_ge(dec_var, 1)
            nc.gpsimd.tensor_tensor(dec[:, 4, 0:NS * NH], dec[:, 3, 0:NS * NH], half[:, 0:NS * NH], ALU.pow).then_inc(dec_rs, 1)

        @block.scalar
        def _(act):
            def split_hi(pair, par):
                act.wait_ge(w_in_s[par], 16 * (pair + 1))
                if not (isinstance(pair, int) and pair == 0):
                    act.wait_ge(done, NTILE * (2 * pair + par - 1))
                nc.scalar.activation(WH[:, par], WS[:, par], ACT.Copy).then_inc(w_hi, 1)

            split_hi(0, 0)
            fl, fa = tk["f_log"], tk["f_abs"]
            act.wait_ge(biased, 1)
            nc.scalar.activation(fa[:, :], fl[:, :], ACT.Abs)
            nc.scalar.activation(sm[:, 9, :], sm[:, 2, :], ACT.Abs).then_inc(act_own, 1)
            act.wait_ge(act_own, 1)
            nc.scalar.activation(fa[:, :], fa[:, :], ACT.Exp, scale=-1.0)
            nc.scalar.activation(sm[:, 9, :], sm[:, 9, :], ACT.Exp, scale=-1.0).then_inc(act_own, 1)
            act.wait_ge(act_own, 2)
            nc.scalar.activation(fa[:, :], fa[:, :], ACT.Ln, bias=1.0)
            nc.scalar.activation(sm[:, 9, :], sm[:, 9, :], ACT.Ln, bias=1.0).then_inc(softplus, 1)
            act.wait_ge(exps_in, 1)
            nc.scalar.activation(tk["exp_negm"][:, :], tk["exp_negm"][:, :], ACT.Exp, scale=-1.0)
            nc.scalar.activation(tk["w_end"][:, :], tk["w_end"][:, :], ACT.Exp)
            nc.scalar.activation(tk["f_end"][:, :], tk["f_end"][:, :], ACT.Exp)
            nc.scalar.activation(sm[:, 4, :], sm[:, 3, :], ACT.Exp, scale=-1.0)
            nc.scalar.activation(sm[:, 5:7, :], sm[:, 5:7, :], ACT.Exp).then_inc(exps_set, 1)

            def tiles_of(pair, par):
                for t, (c0, n) in enumerate(TILES):
                    j = par * NTILE + t
                    act.wait_ge(done, 2 * NTILE * pair + j + 1)
                    yield t, j % 2, c0, n

            def tanh_z(pair, par, t):
                c0, n = TILES[t]
                b = (par * NTILE + t) % 2
                act.wait_ge(done, 2 * NTILE * pair + par * NTILE + t + 1)
                nc.scalar.activation(ZT[:, b, 0:n], G[b][:, 0:n], ACT.Tanh, scale=0.5).then_inc(z_set, 1)

            with act.Fori(0, NP1) as h:
                pair = F1 + h
                split_hi(pair, 1)
                act.wait_ge(row_out[0], 16 * h)
                for t, b, c0, n in tiles_of(pair, 0):
                    nc.scalar.activation(E0[:, c0:c0 + n], G[b][:, 0:n], ACT.Copy).then_inc(free[b], 1)
                split_hi(pair + 1, 0)
                act.wait_ge(row_out[1], 16 * h)
                for t, b, c0, n in tiles_of(pair, 1):
                    nc.scalar.activation(E1[:, c0:c0 + n], G[b][:, 0:n], ACT.Copy, scale=QSCALE).then_inc(free[b], 1)

            act.wait_ge(row_out[0], 16 * NP1)
            with act.Fori(0, NP2) as i:
                pair = F2 + i
                split_hi(pair, 1)
                act.wait_ge(gate_set, i)
                for t, b, c0, n in tiles_of(pair, 0):
                    nc.scalar.activation(E0[:, c0:c0 + n], G[b][:, 0:n], ACT.Tanh, scale=0.5).then_inc(free[b], 1)
                split_hi(pair + 1, 0)
                for t in range(NTILE):
                    tanh_z(pair, 1, t)

            def chunk_act(c, s):
                if s == 0:
                    act.wait_ge(kq_in, 48 * (c + 1))
                    act.wait_ge(num_done, NH * c)
                    for h in range(NH):
                        last = nc.scalar.activation(QW[:, h, :], nM[:, h, :], ACT.Exp, bias=tk["m_prev"][:, bass.ds(NH * c + h, 1)])
                    last.then_inc(wint_set, 1)
                    act.wait_ge(dpre, c + 1)
                    for h in range(NH):
                        last = nc.scalar.activation(Dm[:, h, :], Dm[:, h, :], ACT.Exp, bias=tk["a_in"][:, bass.ds(NH * c + h, 1)])
                    last.then_inc(dexp_set, 1)
                elif 2 <= s < 2 + NH:
                    h = s - 2
                    act.wait_ge(sq_set, NH * c + h)
                    act.wait_ge(h_set, NH * c + h + 3)
                    nc.scalar.activation(Dm[:, 0:2, :].rearrange("p a b -> p (a b)"), HB[:, h, :], ACT.Square,
                                         accum_out=ss[:, 0, h:h + 1]).then_inc(sq_set, 1)

            with act.Fori(0, KB) as i:
                pair = F3 + 2 * i
                split_hi(pair, 1)
                act.wait_ge(u_used, i + 1)
                act.wait_ge(conv_out, 32 * i)
                for s in range(NTILE):
                    chunk_act(2 * i, s)
                    c0, n = TILES[s]
                    act.wait_ge(done, 2 * NTILE * pair + s + 1)
                    nc.scalar.activation(E0[:, 2 + c0:2 + c0 + n], G[s % 2][:, 0:n], ACT.Copy).then_inc(free[s % 2], 1)
                split_hi(pair + 1, 0)
                for s in range(NTILE):
                    chunk_act(2 * i, NTILE + s)
                split_hi(pair + 1, 1)
                for s in range(NTILE):
                    chunk_act(2 * i + 1, s)
                    tanh_z(pair + 1, 0, s)
                split_hi(pair + 2, 0)
                for s in range(NTILE):
                    chunk_act(2 * i + 1, NTILE + s)

            def gate_rows(i, last=False):
                pair = F4 + i
                split_hi(pair, 1)
                act.wait_ge(row_out[0], 16 * (row_tm + i))
                for t, b, c0, n in tiles_of(pair, 0):
                    nc.scalar.activation(E0[:, c0:c0 + n], G[b][:, 0:n], ACT.Tanh, scale=0.5).then_inc(free[b], 1)
                if not last:
                    split_hi(pair + 1, 0)
                act.wait_ge(row_out[1], 16 * (row_tc + i))
                for t, b, c0, n in tiles_of(pair, 1):
                    nc.scalar.activation(E1[:, c0:c0 + n], G[b][:, 0:n], ACT.Tanh, scale=0.5).then_inc(free[b], 1)

            act.wait_ge(u_used, KB + 1)
            act.wait_ge(conv_out, 32 * KB)
            with act.Fori(0, NP4 - 1) as i:
                gate_rows(i)
            gate_rows(NP4 - 1, True)

        @block.vector
        def _(dve):
            own = Chain(dve, dve_own)
            link = own.link

            def split_lo(pair, par):
                dve.wait_ge(w_hi, 2 * pair + par + 1)
                nc.vector.tensor_tensor(WL[:, par], WS[:, par], WH[:, par].bitcast(F32), ALU.subtract).then_inc(w_ready, 1)

            nc.vector.memset(ss[:, :, :], 0.0).then_inc(free[0], 1)
            nc.vector.memset(den[:, :, :], 0.0).then_inc(free[1], 1)
            nc.vector.memset(rowA[:, :, :], 0.0).then_inc(h_set, 2)
            nc.vector.memset(CS[:, :, :], 0.0).then_inc(c_set, NH)
            split_lo(0, 0)
            dve.wait_ge(const_in, 144)
            f3 = tk["f_log"][:, :].rearrange("p (c h) -> p c h", h=NH)
            a3 = tk["a_in"][:, :].rearrange("p (c h) -> p c h", h=NH)
            bi = bif[:, 0:NH].unsqueeze(1).to_broadcast([P, NCH, NH])
            bf = bif[:, NH:2 * NH].unsqueeze(1).to_broadcast([P, NCH, NH])
            nc.vector.tensor_tensor(a3, g.IF[:, 0:NCH, 0:NH], bi, ALU.add)
            nc.vector.tensor_tensor(f3, g.IF[:, 0:NCH, NH:2 * NH], bf, ALU.add)
            nc.vector.tensor_tensor(sm[:, 1, :], g.IF[:NS, NCH, 0:NH], bif[:NS, 0:NH], ALU.add)
            nc.vector.tensor_tensor(sm[:, 2, :], g.IF[:NS, NCH, NH:2 * NH], bif[:NS, NH:2 * NH], ALU.add).then_inc(biased, 1)
            nc.vector.tensor_scalar(hnw[:, :], hnw[:, :], 0.25, None, ALU.mult)
            link(nc.vector.tensor_scalar(cw[:, :, :], cw[:, :, :], 0.5, None, ALU.mult))
            dve.wait_ge(softplus, 1)
            nc.vector.scalar_tensor_tensor(out=tk["f_log"][:, :], in0=tk["f_log"][:, :], scalar=0.0, in1=tk["f_abs"][:, :],
                                           op0=ALU.min, op1=ALU.subtract).then_inc(lf_set, 1)
            link(nc.vector.scalar_tensor_tensor(out=sm[:, 8, :], in0=sm[:, 2, :], scalar=0.0, in1=sm[:, 9, :],
                                                op0=ALU.min, op1=ALU.subtract))
            link(nc.vector.tensor_tensor(sm[:, 5, :], sm[:, 8, :], sm[:, 0, :], ALU.add))
            link(nc.vector.tensor_tensor(sm[:, 3, :], sm[:, 5, :], sm[:, 1, :], ALU.max))
            link(nc.vector.tensor_tensor(sm[:, 5, :], sm[:, 5, :], sm[:, 3, :], ALU.subtract))
            link(nc.vector.tensor_tensor(sm[:, 6, :], sm[:, 1, :], sm[:, 3, :], ALU.subtract))
            dve.wait_ge(b_mm, 1)
            nc.vector.tensor_copy(tk["b_cum"][:, :], PS[:, 0, 0:HC])
            nc.vector.tensor_copy(rowA[0:1, 1, 0:HC], PS[0:1, 1, 0:HC])
            nc.vector.tensor_copy(cs[:, :, :], PN[0][:, 0:2 * NS * KB].rearrange("p (k n) -> p k n", k=KB))
            nc.vector.tensor_tensor(tk["a_in"][:, :], tk["a_in"][:, :], PS[:, 0, 0:HC], ALU.subtract).then_inc(a_set, 1)
            dve.wait_ge(a_mm, 1)
            link(nc.vector.tensor_copy(aT, PT[0][0:HC, 0, :]))
            nc.vector.tensor_tensor_scan(cM, aT, aT, -BIG, ALU.max, ALU.max).then_inc(cm_set, 1)
            dve.wait_ge(al_mm, 1)
            link(nc.vector.tensor_copy(rowA[0:1, 0, 0:HC], PS[0:1, 2, 0:HC]))
            for h in range(NH):
                last = nc.vector.tensor_tensor_scan(rowA[0:1, 2, NH + h:NH + HC:NH], rowA[0:1, 0, h:HC:NH],
                                                    rowA[0:1, 1, h:HC:NH], 0.0, ALU.max, ALU.add)
            link(last)
            nc.vector.tensor_tensor(rowA[0:1, 3, 0:HC], rowA[0:1, 2, 0:HC], rowA[0:1, 0, 0:HC], ALU.max).then_inc(m_set, 1)
            dve.wait_ge(m_mm, 1)
            nc.vector.tensor_copy(tk["m_prev"][:, :], PT[1][:, 0, 0:HC])
            nc.vector.tensor_tensor(tk["w_end"][:, :], tk["a_in"][:, :], PT[1][:, 1, 0:HC], ALU.subtract)
            link(nc.vector.tensor_copy(col[:, :], PT[1][0:HC, 2, 0:1]))
            nc.vector.tensor_tensor(tk["f_end"][:, :], tk["m_prev"][:, :], PT[1][:, 1, 0:HC], ALU.subtract)
            link(nc.vector.tensor_scalar(cM, cM, col[:, 0:1], None, ALU.max))
            nc.vector.tensor_scalar(aT, cM, -1.0, None, ALU.mult).then_inc(M_set, 1)
            dve.wait_ge(mt_mm, 1)
            nc.vector.tensor_tensor(tk["exp_negm"][:, :], tk["b_cum"][:, :], PT[0][:, 0, 0:HC], ALU.add).then_inc(exps_in, 1)

            with dve.Fori(0, NP1) as h:
                split_lo(F1 + h, 1)
                split_lo(F1 + h + 1, 0)

            def silu_z(pair, par, t, zn):
                c0, n = TILES[t]
                b = (par * NTILE + t) % 2
                dve.wait_ge(z_set, zn)
                nc.vector.scalar_tensor_tensor(out=E1[:, c0:c0 + n], in0=ZT[:, b, 0:n], scalar=1.0, in1=G[b][:, 0:n],
                                               op0=ALU.add, op1=ALU.mult).then_inc(free[b], 1)

            with dve.Fori(0, NP2) as i:
                own.enter(i, 1)
                pair = F2 + i
                split_lo(pair, 1)
                split_lo(pair + 1, 0)
                dve.wait_ge(row_out[1], 16 * (row_gate + i))
                for t in range(NTILE):
                    silu_z(pair, 1, t, NTILE * i + t + 1)
                block_waits(dve, pair, 1)
                link(nc.vector.scalar_tensor_tensor(out=E1[:, 0:T], in0=E0[:, 0:T], scalar=1.0, in1=E1[:, 0:T],
                                                    op0=ALU.add, op1=ALU.mult))
                nc.vector.tensor_scalar(E1[:, 0:T], E1[:, 0:T], hnw[:, bass.ds(i, 1)], None, ALU.mult).then_inc(gate_set, 1)
            own.leave(NP2)
            nc.vector.memset(E0[:, 0:2], 0.0).then_inc(u_used, 1)

            def chunk_dve(c, s):
                if s == 0:
                    dve.wait_ge(kq_in, 48 * (c + 1))
                    dve.wait_ge(sq_set, NH * c)
                    nc.vector.tensor_tensor(Dm[:, :, :], nM[:, :, :], mask[:, :].unsqueeze(1).to_broadcast([P, NH, P]),
                                            ALU.min).then_inc(dpre, 1)
                    dve.wait_ge(kt_done, c + 1)
                    dve.wait_ge(cu_done, NH * c)
                    nc.vector.tensor_tensor(KW[:, :, :], PT[0][:, :, :], bc(tk["w_end"][:, bass.ds(NH * c, NH)], P),
                                            ALU.mult).then_inc(kw_set, 1)
                    dve.wait_ge(wint_set, c + 1)
                    nc.vector.tensor_tensor(QW[:, :, :], QW[:, :, :], qT[:, :, :], ALU.mult).then_inc(qw_set, 1)
                    dve.wait_ge(s_done, c + 1)
                    dve.wait_ge(dexp_set, c + 1)
                    dve.wait_ge(num_done, NH * c)
                    nc.vector.tensor_tensor(PT_[:, :, :], PS[:, :, :], Dm[:, :, :], ALU.mult).then_inc(p_set, 1)
                elif 2 <= s < 2 + NH:
                    h = s - 2
                    ch = bass.ds(NH * c + h, 1)
                    dve.wait_ge(num_done, NH * c + h + 1)
                    link(nc.vector.tensor_scalar(den[:, 0, 0:1], PN[h % 2][:, DHV:DHV + 1], -1.0, tk["exp_negm"][:, ch],
                                                 ALU.mult, ALU.max))
                    link(nc.vector.tensor_tensor(den[:, 0, 1:2], PN[h % 2][:, DHV:DHV + 1], den[:, 0, 0:1], ALU.max))
                    link(nc.vector.reciprocal(den[:, 1, 0:1], den[:, 0, 1:2]))
                    if h == 0:
                        dve.wait_ge(ht_done, c)
                    nc.vector.tensor_scalar(HB[:, h, :], PN[h % 2][:, 0:DHV], den[:, 1, 0:1], None, ALU.mult).then_inc(h_set, 1)
                    dve.wait_ge(cu_done, NH * c + h + 1)
                    nc.vector.scalar_tensor_tensor(out=CS[:, h, :], in0=CS[:, h, :], scalar=tk["f_end"][:, ch], in1=PC[:, 0:DHV + 1],
                                                   op0=ALU.mult, op1=ALU.add).then_inc(c_set, 1)
                elif s == 6:
                    dve.wait_ge(sq_set, NH * (c + 1))
                    nc.vector.tensor_scalar(ss[:, 1, :], ss[:, 0, :], 1.0 / DHV, EPS, ALU.mult, ALU.add).then_inc(var_set, 1)
                elif s == 7:
                    dve.wait_ge(rs_set, c + 1)
                    nc.vector.tensor_tensor(HB[:, :, :], HB[:, :, :], bc(ss[:, 2, :], DHV), ALU.mult).then_inc(hn_set, 1)
                elif s == 8:
                    dve.wait_ge(ht_done, c + 1)
                    dve.wait_ge(gate_in, 16 * (c + 1))
                    nc.vector.tensor_tensor(GT[:, 0:4, :], GT[:, 0:4, :], PT[0][:, :, :], ALU.mult)
                    nc.vector.tensor_tensor(GT[:, 4:8, :], GT[:, 4:8, :], PT[1][:, :, :], ALU.mult).then_inc(hg_set, 1)

            def conv_tile(i, t):
                c0, n = TILES[t]
                w = [cw[:, j, bass.ds(i, 1)] for j in range(CW)]
                m = min(n, L - c0)
                link(nc.vector.tensor_scalar(CV[:, 0:n], E0[:, 2 + c0:2 + c0 + n], w[2], None, ALU.mult))
                link(nc.vector.scalar_tensor_tensor(out=CV[:, 0:m], in0=E0[:, 1 + c0:1 + c0 + m], scalar=w[1], in1=CV[:, 0:m],
                                                    op0=ALU.mult, op1=ALU.add))
                if m < n:
                    st = cs[:, bass.ds(i, 1), :].rearrange("p a (b r) -> p (a b) r", r=2)
                    for r in range(2):
                        link(nc.vector.scalar_tensor_tensor(out=CV[:, m:n], in0=st[:, :, r], scalar=w[r], in1=CV[:, m:n],
                                                            op0=ALU.mult, op1=ALU.add))
                ins = nc.vector.scalar_tensor_tensor(out=CV[:, 0:m], in0=E0[:, c0:c0 + m], scalar=w[0], in1=CV[:, 0:m],
                                                     op0=ALU.mult, op1=ALU.add)
                return ins

            with dve.Fori(0, KB) as i:
                own.enter(i, 6 * NH + 4 * NTILE + 1)
                pair = F3 + 2 * i
                split_lo(pair, 1)
                for s in range(NTILE):
                    chunk_dve(2 * i, s)
                split_lo(pair + 1, 0)
                for s in range(NTILE):
                    chunk_dve(2 * i, NTILE + s)
                    if s == 0:
                        block_waits(dve, pair, 0)
                    c0, n = TILES[s]
                    b = (NTILE + s) % 2
                    dve.wait_ge(done, 2 * NTILE * pair + NTILE + s + 1)
                    nc.vector.tensor_tensor(E0[:, 2 + c0:2 + c0 + n], E0[:, 2 + c0:2 + c0 + n], G[b][:, 0:n], ALU.mult).then_inc(free[b], 1)
                split_lo(pair + 1, 1)
                dve.wait_ge(row_out[1], 16 * (row_conv + i))
                for s in range(NTILE):
                    chunk_dve(2 * i + 1, s)
                    silu_z(pair + 1, 0, s, NTILE * (NP2 + i) + s + 1)
                split_lo(pair + 2, 0)
                for s in range(NTILE):
                    chunk_dve(2 * i + 1, NTILE + s)
                    if s == 0:
                        block_waits(dve, pair, 1)
                        block_waits(dve, pair + 1, 0)
                    else:
                        dve.wait_ge(free[(NTILE + s - 1) % 2], NTILE * (pair + 1) + (NTILE + s - 1) // 2 + 2)
                    ins = conv_tile(i, s)
                    if s == NTILE - 1:
                        ins.then_inc(u_used, 1)
                        dve.wait_ge(u_used, i + 2)
                    else:
                        link(ins)
                    c0, n = TILES[s]
                    b = (NTILE + s) % 2
                    link(nc.vector.tensor_tensor(CV[:, 0:n], CV[:, 0:n], E1[:, c0:c0 + n], ALU.mult))
                    dve.wait_ge(done, 2 * NTILE * (pair + 1) + NTILE + s + 1)
                    nc.vector.tensor_tensor(E1[:, c0:c0 + n], CV[:, 0:n], G[b][:, 0:n], ALU.mult).then_inc(free[b], 1)
            own.leave(KB)

            dve.wait_ge(ct_mm, 1)
            HB8 = HB[:, :, :].rearrange("p h (a d) -> p (h a) d", a=2)
            nc.vector.tensor_copy(HB8[:, 0:4, :], PT[0][:, :, :])
            nc.vector.tensor_copy(HB8[:, 4:8, :], PT[1][:, :, :]).then_inc(ct_set, 1)
            split_lo(F4, 1)
            split_lo(F4 + 1, 0)
            dve.wait_ge(dec_mm, 1)
            nc.vector.tensor_copy(PT_[:NS, :, :], PS[:NS, :, :])
            nc.vector.tensor_copy(KW[:NS, :, :].rearrange("p h d -> p (h d)"), PN[0][:NS, :])
            vd = dec[:, 5, :]
            link(nc.vector.tensor_copy(vd.rearrange("p (b k) -> p k b", k=KB), PN[1][:, 0:KB * NS].rearrange("p (k b) -> p k b", k=KB)))
            link(nc.vector.tensor_tensor(Dm[:NS, :, :], KW[:NS, :, :], bc(sm[:, 6, :], P), ALU.mult))
            link(nc.vector.tensor_tensor(QW[:NS, :, :], QW[:NS, :, :], bc(sm[:, 5, :], P), ALU.mult))
            link(nc.vector.tensor_tensor(QW[:NS, :, :], QW[:NS, :, :], Dm[:NS, :, :], ALU.add))
            link(nc.vector.tensor_tensor(Dm[:NS, :, :], QW[:NS, :, :], PT_[:NS, :, :], ALU.mult))
            link(nc.vector.tensor_reduce(sm[:, 8, :], Dm[:NS, :, :], AX.X, ALU.add))
            link(nc.vector.scalar_tensor_tensor(out=sm[:, 9, :], in0=sm[:, 8, :], scalar=-1.0, in1=sm[:, 4, :],
                                                op0=ALU.mult, op1=ALU.max))
            link(nc.vector.tensor_tensor(sm[:, 9, :], sm[:, 9, :], sm[:, 8, :], ALU.max))
            nc.vector.reciprocal(sm[:, 7, :], sm[:, 9, :]).then_inc(dec_rows, 1)
            dve.wait_ge(dec_bc, 32)
            vd3 = vd.rearrange("p (n a) -> p n a", a=2)
            link(nc.vector.tensor_tensor(vd3, vd3, bc(dec[:, 0, NS * NH:2 * NS * NH], 2), ALU.mult))
            dve.wait_ge(c_out, 16 * 5)

            def decode(b):
                dve.wait_ge(dec_kq_in, 32 * (b + 1))
                dve.wait_ge(dec_c_in, 16 * (b + 1))
                GT4 = GT[:, :, :].rearrange("p (h a) d -> p h (a d)", a=2)
                link(nc.vector.tensor_tensor(GT4, GT4, bc(dec[:, 0, sl(b, NH)], 2 * P), ALU.mult))
                vb = dec[:, 5, sl(b, KB)].rearrange("p (h a) -> p h a", a=2)
                for a in range(2):
                    last = nc.vector.tensor_tensor(HB[:, :, a * P:(a + 1) * P], kT[:, :, :], bc(vb[:, :, a], P), ALU.mult)
                link(last)
                link(nc.vector.tensor_tensor(GT[:, :, :], GT[:, :, :], HB8, ALU.add))
                for a in range(2):
                    last = nc.vector.tensor_tensor(HB[:, :, a * P:(a + 1) * P], qT[:, :, :], GT4[:, :, a * P:(a + 1) * P], ALU.mult)
                link(last)
                nc.vector.tensor_reduce(dec[:, 2, sl(b, KB)], HB8, AX.X, ALU.add).then_inc(dec_upd, 1)

            with dve.Fori(0, NP4 - 2) as i:
                own.enter(i, 4)
                split_lo(F4 + i + 1, 1)
                decode(i)
                split_lo(F4 + i + 2, 0)
            own.leave(NP4 - 2)
            split_lo(NPAIR - 1, 1)
            decode(NS - 2)
            decode(NS - 1)
            dve.wait_ge(dec_upd, NS)
            num3 = dec[:, 2, :].rearrange("p (n a) -> p n a", a=2)
            link(nc.vector.tensor_tensor(num3, num3, bc(dec[:, 1, 0:NS * NH], 2), ALU.mult))
            nc.vector.tensor_tensor(dec[:, 3, :], dec[:, 2, :], dec[:, 2, :], ALU.mult).then_inc(dec_sq, 1)
            dve.wait_ge(dec_sum, 1)
            link(nc.vector.tensor_reduce(dec[:, 4, 0:NS * NH], PN[0][:, 0:2 * NS * NH].rearrange("p (n a) -> p n a", a=2), AX.X, ALU.add))
            nc.vector.tensor_scalar(dec[:, 3, 0:NS * NH], dec[:, 4, 0:NS * NH], 1.0 / DHV, EPS, ALU.mult, ALU.add).then_inc(dec_var, 1)
            dve.wait_ge(dec_rs, 1)
            link(nc.vector.tensor_tensor(num3, num3, bc(dec[:, 4, 0:NS * NH], 2), ALU.mult))
            nc.vector.tensor_tensor(dec[:, 6, :].rearrange("p (k b) -> p b k", k=KB), dec[:, 2, :].rearrange("p (b k) -> p b k", k=KB),
                                    dec[:, 7, :].rearrange("p (k b) -> p b k", k=KB), ALU.mult).then_inc(dec_h, 1)

        @block.tensor
        def _(pe):
            def tile(pair, par, t):
                c0, n = TILES[t]
                j = par * NTILE + t
                if t == 0:
                    pe.wait_ge(w_ready, 2 * pair + par + 1)
                pe.wait_ge(free[j % 2], NTILE * pair + j // 2 + 1)
                step = 0
                for k in range(KB):
                    for w, x in ((WH, g.RH), (WH, g.RL), (WL, g.RH)):
                        last = nc.tensor.matmul(G[j % 2][:, 0:n], w[:, par, k, :], x[:, k, c0:c0 + n],
                                                start=(step == 0), stop=(step == 3 * KB - 1))
                        step += 1
                last.then_inc(done, 1)

            pe.wait_ge(const_set, 6)
            pe.wait_ge(const_in, 144)
            for k in range(KB):
                src = (csr if k < 4 else csr2)[:, (k % 4) * P:(k % 4 + 1) * P]
                nc.tensor.transpose(PN[0][:, k * 2 * NS:(k + 1) * 2 * NS], src, g.ident[:2 * NS, :2 * NS])
            pe.wait_ge(lf_set, 1)
            nc.tensor.matmul(PS[:, 0, 0:HC], cumU[:, :], tk["f_log"][:, :], start=True, stop=True)
            nc.tensor.matmul(PS[0:1, 1, 0:HC], ones[:, 0:1], tk["f_log"][:, :], start=True, stop=True).then_inc(b_mm, 1)
            pe.wait_ge(a_set, 1)
            nc.tensor.transpose(PT[0][0:HC, 0, :], tk["a_in"][:, :], g.ident[:, :]).then_inc(a_mm, 1)
            pe.wait_ge(cm_set, 1)
            nc.tensor.matmul(PS[0:1, 2, 0:HC], cM[:, P - 1:P], g.ident[0:HC, 0:HC], start=True, stop=True).then_inc(al_mm, 1)
            pe.wait_ge(m_set, 1)
            nc.tensor.matmul(PT[1][:, 0, 0:HC], ones[0:1, :], rowA[0:1, 2, 0:HC], start=True, stop=True)
            nc.tensor.matmul(PT[1][:, 1, 0:HC], ones[0:1, :], rowA[0:1, 3, 0:HC], start=True, stop=True)
            nc.tensor.matmul(PT[1][0:HC, 2, 0:1], rowA[0:1, 2, 0:HC], ones[0:1, 0:1], start=True, stop=True).then_inc(m_mm, 1)
            pe.wait_ge(M_set, 1)
            nc.tensor.transpose(PT[0][:, 0, 0:HC], cM, g.ident[0:HC, 0:HC]).then_inc(mt_mm, 1)

            with pe.Fori(0, NP1 + NP2) as i:
                for par in range(2):
                    for t in range(NTILE):
                        tile(i, par, t)

            def chunk_pe(c, s):
                if s == 0:
                    pe.wait_ge(kq_in, 48 * (c + 1))
                    pe.wait_ge(p_set, c)
                    for h in range(NH):
                        last = nc.tensor.matmul(PS[:, h, :], kT[:, h, :], qT[:, h, :], start=True, stop=True)
                    last.then_inc(s_done, 1)
                    pe.wait_ge(hg_set, c)
                    for h in range(NH):
                        last = nc.tensor.transpose(PT[0][:, h, :], kT[:, h, :], g.ident[:, :])
                    last.then_inc(kt_done, 1)
                elif 2 <= s < 2 + NH:
                    h = s - 2
                    if h == 0:
                        pe.wait_ge(v_in, 16 * (c + 1))
                        pe.wait_ge(p_set, c + 1)
                        pe.wait_ge(qw_set, c + 1)
                        pe.wait_ge(kw_set, c + 1)
                    pe.wait_ge(h_set, NH * c + h + 1)
                    pe.wait_ge(c_set, NH * c + h + 1)
                    nc.tensor.matmul(PN[h % 2][:, 0:DHV + 1], PT_[:, h, :], va[:, h, :], start=True, stop=False)
                    nc.tensor.matmul(PN[h % 2][:, 0:DHV + 1], QW[:, h, :], CS[:, h, :], start=False, stop=True).then_inc(num_done, 1)
                    pe.wait_ge(c_set, NH * c + h + NH)
                    nc.tensor.matmul(PC[:, 0:DHV + 1], KW[:, h, :], va[:, h, :], start=True, stop=True).then_inc(cu_done, 1)
                elif s == 8:
                    pe.wait_ge(hn_set, c + 1)
                    for k in range(KB):
                        last = nc.tensor.transpose(PT[k // 4][:, k % 4, :], HB[:, k // 2, (k % 2) * P:(k % 2 + 1) * P], g.ident[:, :])
                    last.then_inc(ht_done, 1)

            with pe.Fori(0, KB) as i:
                for q in range(4):
                    for t in range(NTILE):
                        chunk_pe(2 * i + q // 2, (q % 2) * NTILE + t)
                        tile(F3 + 2 * i + q // 2, q % 2, t)

            pe.wait_ge(c_set, HC + NH)
            pe.wait_ge(hg_set, NCH)
            for k in range(KB):
                last = nc.tensor.transpose(PT[k // 4][:, k % 4, :], CS[:, k // 2, (k % 2) * P:(k % 2 + 1) * P], g.ident[:, :])
            last.then_inc(ct_mm, 1)

            for t in range(2 * NTILE):
                tile(F4, t // NTILE, t % NTILE)
            pe.wait_ge(dec_in, 80)
            for h in range(NH):
                nc.tensor.transpose(PS[0:NS, h, :], GT[:, 0, h * NS:(h + 1) * NS], g.ident[:, :])
                nc.tensor.transpose(PN[0][0:NS, h * P:(h + 1) * P], GT[:, 0, (NH + h) * NS:(NH + h + 1) * NS], g.ident[:, :])
            for k in range(KB):
                last = nc.tensor.transpose(PN[1][:, k * NS:(k + 1) * NS], va[0:NS, k // 2, (k % 2) * P:(k % 2 + 1) * P], g.ident[0:NS, 0:NS])
            last.then_inc(dec_mm, 1)
            with pe.Fori(1, NP4) as i:
                for t in range(2 * NTILE):
                    tile(F4 + i, t // NTILE, t % NTILE)
            pe.wait_ge(dec_sq, 1)
            nc.tensor.matmul(PN[0][:, 0:2 * NS * NH], ones[:, :], dec[:, 3, :], start=True, stop=True).then_inc(dec_sum, 1)

    ctx.close()


def phase_c(nc, g):
    ctx = ExitStack()
    sem = lambda n: ctx.enter_context(nc.semaphore("c_" + n))
    NO = KB
    NB = 4
    AH = [sbuf(nc, ctx, f"act_hi{j}", [P, KB, TN], F32R) for j in range(2)]
    AL = [sbuf(nc, ctx, f"act_lo{j}", [P, KB, TN], F32R) for j in range(2)]
    ST = [sbuf(nc, ctx, f"act_stage{j}", [P, KB, TN]) for j in range(2)]
    TG = [sbuf(nc, ctx, f"tanh_gate{j}", [P, KB, TN]) for j in range(2)]
    MX = sbuf(nc, ctx, "mix", [P, KB, TN])
    TMP = sbuf(nc, ctx, "c_part", [P, 2, TN])
    G = [psum(nc, ctx, f"c_g{j}", [P, 512]) for j in range(NB)]
    WSG = [TG[j][:, :, :].rearrange("p k n -> p (k n)")[:, 0:2 * D] for j in range(2)]

    w_in_s = [sem("w_in0"), sem("w_in1")]
    w_hi, w_ready = sem("w_hi"), sem("w_ready")
    st_in = [sem("st_in0"), sem("st_in1")]
    tg_in = [sem("tg_in0"), sem("tg_in1")]
    a_hi = [sem("a_hi0"), sem("a_hi1")]
    a_ready = [sem("a_ready0"), sem("a_ready1")]
    done, free, own_s = sem("tile_done"), sem("bank_free"), sem("dve_own")
    mix_set, mix_out = sem("mix_set"), sem("mix_out")

    acts = [g.hg_d, g.cv_d]
    tanhs = [g.tm_d, g.tc_d]
    wts = [g.w_proj_m[0].rearrange("(k p) n -> k p n", p=P), g.w_proj_c[0].rearrange("(k p) n -> k p n", p=P)]

    def cols(t):
        return slice(t * TN, t * TN + TN) if isinstance(t, int) else bass.ds(t * TN, TN)

    with nc.Block() as block:

        @block.sync
        def _(sp):
            def load_act(t, br):
                if not (isinstance(t, int) and t == 0):
                    sp.wait_ge(a_ready[br], t)
                sp.dma_start(ST[br][:, :, :], acts[br][:, :, cols(t)].rearrange("k p n -> p k n")).then_inc(st_in[br], 16)

            def load_tanh(t, br):
                if not (isinstance(t, int) and t == 0):
                    sp.wait_ge(free, 2 * NO * (t - 1) + NO * (br + 1) + NB)
                sp.dma_start(TG[br][:, :, :], tanhs[br][:, :, cols(t)].rearrange("k p n -> p k n")).then_inc(tg_in[br], 16)

            for k in range(KB):
                if k >= 2:
                    sp.wait_ge(w_ready, k - 1)
                for br in range(2):
                    sp.dma_start(WSG[k % 2][:, br * D:(br + 1) * D], wts[br][k]).then_inc(w_in_s[k % 2], 16)
                if k < 2:
                    load_act(0, k)
            sp.wait_ge(w_ready, KB)
            load_tanh(0, 0)
            load_tanh(0, 1)

            def body(t, last=False):
                if not last:
                    load_act(t + 1, 0)
                    load_act(t + 1, 1)
                    load_tanh(t + 1, 0)
                sp.wait_ge(mix_set, t + 1)
                sp.dma_start(g.mix_d[:, :, cols(t)].rearrange("k p n -> p k n"), MX[:, :, :]).then_inc(mix_out, 16)
                if not last:
                    load_tanh(t + 1, 1)

            with sp.Fori(0, NTC - 1) as t:
                body(t)
            body(NTC - 1, True)
            sp.wait_ge(mix_out, 16 * NTC)

        @block.scalar
        def _(act):
            def split_hi(t, br):
                act.wait_ge(st_in[br], 16 * (t + 1))
                if not (isinstance(t, int) and t == 0):
                    act.wait_ge(done, 2 * NO * (t - 1) + NO * (br + 1))
                nc.scalar.activation(AH[br][:, :, :], ST[br][:, :, :], ACT.Copy).then_inc(a_hi[br], 1)

            for k in range(KB):
                act.wait_ge(w_in_s[k % 2], 32 * (k // 2 + 1))
                nc.scalar.activation(g.RH[:, k, 0:2 * D], WSG[k % 2], ACT.Copy).then_inc(w_hi, 1)
                if k == 0:
                    split_hi(0, 0)
            split_hi(0, 1)
            with act.Fori(1, NTC) as t:
                split_hi(t, 0)
                split_hi(t, 1)

        @block.vector
        def _(dve):
            own = Chain(dve, own_s)

            def split_lo(t, br):
                dve.wait_ge(a_hi[br], t + 1)
                nc.vector.tensor_tensor(AL[br][:, :, :], ST[br][:, :, :], AH[br][:, :, :].bitcast(F32),
                                        ALU.subtract).then_inc(a_ready[br], 1)

            nc.vector.memset(TMP[:, :, :], 0.0).then_inc(free, NB)
            for k in range(KB):
                dve.wait_ge(w_hi, k + 1)
                nc.vector.tensor_tensor(g.RL[:, k, 0:2 * D], WSG[k % 2], g.RHf[:, k, 0:2 * D], ALU.subtract).then_inc(w_ready, 1)
                if k == 0:
                    split_lo(0, 0)
            split_lo(0, 1)

            def body(t, last=False):
                dve.wait_ge(tg_in[0], 16 * (t + 1))
                dve.wait_ge(mix_out, 16 * t)
                for o in range(NO):
                    dve.wait_ge(done, 2 * NO * t + o + 1)
                    nc.vector.scalar_tensor_tensor(out=MX[:, o, :], in0=TG[0][:, o, :], scalar=1.0, in1=G[o % NB][:, 0:TN],
                                                   op0=ALU.add, op1=ALU.mult).then_inc(free, 1)
                if not last:
                    split_lo(t + 1, 0)
                dve.wait_ge(tg_in[1], 16 * (t + 1))
                for o in range(NO):
                    dve.wait_ge(done, 2 * NO * t + NO + o + 1)
                    nc.vector.scalar_tensor_tensor(out=TMP[:, o % 2, :], in0=TG[1][:, o, :], scalar=1.0, in1=G[o % NB][:, 0:TN],
                                                   op0=ALU.add, op1=ALU.mult).then_inc(free, 1)
                    dve.wait_ge(free, 2 * NO * t + NO + o + 1 + NB)
                    ins = nc.vector.tensor_tensor(MX[:, o, :], MX[:, o, :], TMP[:, o % 2, :], ALU.add)
                ins.then_inc(mix_set, 1)
                if not last:
                    split_lo(t + 1, 1)

            with dve.Fori(0, NTC - 1) as t:
                body(t)
            body(NTC - 1, True)

        @block.tensor
        def _(pe):
            pe.wait_ge(w_ready, KB)
            with pe.Fori(0, NTC) as t:
                for br in range(2):
                    pe.wait_ge(a_ready[br], t + 1)
                    for o in range(NO):
                        c0 = br * D + o * P
                        pe.wait_ge(free, 2 * NO * t + br * NO + o + 1)
                        step = 0
                        for k in range(KB):
                            for w, x in ((g.RH, AH[br]), (g.RH, AL[br]), (g.RL, AH[br])):
                                last = nc.tensor.matmul(G[o % NB][:, 0:TN], w[:, k, c0:c0 + P], x[:, k, :],
                                                        start=(step == 0), stop=(step == 3 * KB - 1))
                                step += 1
                        last.then_inc(done, 1)

    ctx.close()


def phase_d(nc, g):
    ctx = ExitStack()
    sem = lambda n: ctx.enter_context(nc.semaphore("d_" + n))
    N = D // 2
    WH, WL = g.RH[:, :, 0:D], g.RL[:, :, 0:D]
    WS = [sbuf(nc, ctx, f"wo_stage{j}", [P, D]) for j in range(2)]
    MS = [sbuf(nc, ctx, f"mix_stage{j}", [P, KB, P]) for j in range(2)]
    MH = [sbuf(nc, ctx, f"mix_hi{j}", [P, KB, P], F32R) for j in range(2)]
    ML = [sbuf(nc, ctx, f"mix_lo{j}", [P, KB, P], F32R) for j in range(2)]
    X = [sbuf(nc, ctx, f"x_res{j}", [P, D]) for j in range(2)]
    Y = [sbuf(nc, ctx, f"y{j}", [P, D]) for j in range(2)]
    junk = sbuf(nc, ctx, "d_junk", [P, D])
    fw = sbuf(nc, ctx, "final_w", [P, D])
    stat = sbuf(nc, ctx, "d_stat", [P, 3, 2])
    half = sbuf(nc, ctx, "d_half", [P, 1])
    G = [psum(nc, ctx, f"d_g{j}", [P, N]) for j in range(4)]

    wo_in = [sem("wo_in0"), sem("wo_in1")]
    w_hi, w_ready = sem("w_hi"), sem("w_ready")
    m_in = [sem("m_in0"), sem("m_in1")]
    x_in = [sem("x_in0"), sem("x_in1")]
    const_in, const_set = sem("const_in"), sem("const_set")
    m_hi, m_ready, done = sem("m_hi"), sem("m_ready"), sem("tile_done")
    summed, squared, var_set, rstd_set, y_set = sem("summed"), sem("squared"), sem("var_set"), sem("rstd_set"), sem("y_set")
    y_out = [sem("y_out0"), sem("y_out1")]

    w_v = g.w_out[0].rearrange("(k p) n -> k p n", p=P)
    xp = g.x_prompt[0].rearrange("(t p) d -> t p d", p=P)
    yp = g.y_prompt[0].rearrange("(t p) d -> t p d", p=P)

    def rows(i):
        return NS if isinstance(i, int) and i == NT - 1 else P

    def at(i):
        return slice(i * P, i * P + rows(i)) if isinstance(i, int) else bass.ds(i * P, P)

    def over_tiles(eng, body):
        with eng.Fori(0, NT // 2) as j:
            body(2 * j, 0)
            body(2 * j + 1, 1)
        body(NT - 1, 0)

    def slot_count(i, par):
        return i + 2 - par

    with nc.Block() as block:

        @block.sync
        def _(sp):
            def load(i, par):
                n = rows(i)
                sp.wait_ge(m_ready, i - 1) if not isinstance(i, int) or i >= 2 else None
                sp.dma_start(MS[par][:, :, 0:n], g.mix_d[:, :, at(i)].rearrange("k p n -> p k n")).then_inc(m_in[par], 16)
                if not isinstance(i, int) or i >= 2:
                    sp.wait_ge(summed, i - 1)
                src = g.x_sample[:, 0, :] if n == NS else (xp[i] if isinstance(i, int) else xp[bass.ds(i, 1)].rearrange("a p d -> (a p) d"))
                sp.dma_start(X[par][:n, :], src).then_inc(x_in[par], 16)

            def store(i, par):
                n = rows(i)
                sp.wait_ge(y_set, i + 1)
                dst = g.y_sample[:, 0, :] if n == NS else (yp[i] if isinstance(i, int) else yp[bass.ds(i, 1)].rearrange("a p d -> (a p) d"))
                sp.dma_start(dst, Y[par][:n, :]).then_inc(y_out[par], 16)

            for k in range(KB):
                if k >= 2:
                    sp.wait_ge(w_ready, k - 1)
                sp.dma_start(WS[k % 2][:, :], w_v[k]).then_inc(wo_in[k % 2], 16)
                if k < 2:
                    load(k, k)
            sp.dma_start(fw[:, :], g.final_norm_w.partition_broadcast(P)).then_inc(const_in, 16)
            with sp.Fori(0, NT // 2 - 1) as j:
                for par in range(2):
                    load(2 * j + par + 2, par)
                    store(2 * j + par, par)
            load(NT - 1, 0)
            store(NT - 3, 0)
            store(NT - 2, 1)
            store(NT - 1, 0)
            sp.wait_ge(y_out[0], 16 * (NT // 2 + 1))
            sp.wait_ge(y_out[1], 16 * (NT // 2))

        @block.gpsimd
        def _(pool):
            nc.gpsimd.memset(half[:, :], -0.5).then_inc(const_set, 1)
            pool.wait_ge(const_set, 1)

            def rstd(i, par):
                n = rows(i)
                pool.wait_ge(var_set, i + 1)
                nc.gpsimd.tensor_tensor(stat[:n, 2, par:par + 1], stat[:n, 1, par:par + 1], half[:n, :], ALU.pow).then_inc(rstd_set, 1)

            over_tiles(pool, rstd)

        def hi(act, i, par):
            n = rows(i)
            act.wait_ge(m_in[par], 8 * slot_count(i, par))
            if not isinstance(i, int) or i >= 2:
                act.wait_ge(done, i - 1)
            nc.scalar.activation(MH[par][:, :, 0:n], MS[par][:, :, 0:n], ACT.Copy).then_inc(m_hi, 1)

        def lo(dve, i, par):
            n = rows(i)
            dve.wait_ge(m_hi, i + 1)
            nc.vector.tensor_tensor(ML[par][:, :, 0:n], MS[par][:, :, 0:n], MH[par][:, :, 0:n].bitcast(F32),
                                    ALU.subtract).then_inc(m_ready, 1)

        def with_lookahead(eng, ahead, finish):
            ahead(eng, 0, 0)
            with eng.Fori(0, NT // 2 - 1) as j:
                for par in range(2):
                    ahead(eng, 2 * j + par + 1, 1 - par)
                    finish(2 * j + par, par)
            for i in range(NT - 3, NT):
                if i + 1 < NT:
                    ahead(eng, i + 1, (i + 1) % 2)
                finish(i, i % 2)

        @block.scalar
        def _(act):
            for k in range(KB):
                act.wait_ge(wo_in[k % 2], 16 * (k // 2 + 1))
                nc.scalar.activation(WH[:, k, :], WS[k % 2][:, :], ACT.Copy).then_inc(w_hi, 1)

            def square(i, par):
                n = rows(i)
                act.wait_ge(summed, i + 1)
                nc.scalar.activation(junk[:n, :], Y[par][:n, :], ACT.Square, accum_out=stat[:n, 0, par:par + 1]).then_inc(squared, 1)

            with_lookahead(act, hi, square)

        @block.vector
        def _(dve):
            for k in range(KB):
                dve.wait_ge(w_hi, k + 1)
                nc.vector.tensor_tensor(WL[:, k, :], WS[k % 2][:, :], g.RHf[:, k, 0:D], ALU.subtract).then_inc(w_ready, 1)
            dve.wait_ge(const_in, 16)

            def finish(i, par):
                n = rows(i)
                dve.wait_ge(x_in[par], 8 * slot_count(i, par))
                dve.wait_ge(done, i + 1)
                if not isinstance(i, int) or i >= 2:
                    dve.wait_ge(y_out[par], 8 * (slot_count(i, par) - 2))
                for j in range(2):
                    last = nc.vector.scalar_tensor_tensor(out=Y[par][:n, j * N:(j + 1) * N], in0=G[2 * par + j][:n, :], scalar=0.5,
                                                          in1=X[par][:n, j * N:(j + 1) * N], op0=ALU.mult, op1=ALU.add)
                last.then_inc(summed, 1)
                dve.wait_ge(squared, i + 1)
                nc.vector.tensor_scalar(stat[:n, 1, par:par + 1], stat[:n, 0, par:par + 1], 1.0 / D, EPS, ALU.mult, ALU.add).then_inc(var_set, 1)
                dve.wait_ge(rstd_set, i + 1)
                nc.vector.scalar_tensor_tensor(out=Y[par][:n, :], in0=Y[par][:n, :], scalar=stat[:n, 2, par:par + 1], in1=fw[:n, :],
                                               op0=ALU.mult, op1=ALU.mult).then_inc(y_set, 1)

            with_lookahead(dve, lo, finish)

        @block.tensor
        def _(pe):
            pe.wait_ge(w_ready, KB)

            def tile(i, par):
                n = rows(i)
                pe.wait_ge(m_ready, i + 1)
                if not isinstance(i, int) or i >= 2:
                    pe.wait_ge(summed, i - 1)
                for j in range(2):
                    step = 0
                    for k in range(KB):
                        for x, w in ((MH, WH), (MH, WL), (ML, WH)):
                            last = nc.tensor.matmul(G[2 * par + j][:n, :], x[par][:, k, 0:n], w[:, k, j * N:(j + 1) * N],
                                                    start=(step == 0), stop=(step == 3 * KB - 1))
                            step += 1
                last.then_inc(done, 1)

            tile(0, 0)
            tile(1, 1)
            with pe.Fori(1, NT // 2) as j:
                tile(2 * j, 0)
                tile(2 * j + 1, 1)
            tile(NT - 1, 0)

    ctx.close()


INPUTS = ["x_prompt", "x_sample", "state_mlstm_C", "state_mlstm_n", "state_mlstm_m", "state_conv", "norm_w", "w_in",
          "b_i", "b_f", "head_norm_w", "conv_w", "w_proj_m", "w_proj_c", "w_out", "final_norm_w"]
OUTPUTS = [("y_prompt", (1, L, D)), ("y_sample", (NS, 1, D)),
           ("new_C_prompt", (1, 1, NH, DHV, DQK)), ("new_n_prompt", (1, 1, NH, DQK)),
           ("new_m_prompt", (1, 1, NH)), ("new_conv_prompt", (1, 1, CW - 1, D)),
           ("new_C_sample", (1, NS, NH, DHV, DQK)), ("new_n_sample", (1, NS, NH, DQK)),
           ("new_m_sample", (1, NS, NH)), ("new_conv_sample", (1, NS, CW - 1, D))]


def kernel(**inputs):
    import concourse.bacc as bacc
    from concourse.bass_utils import run_bass_kernel_spmd

    nc = bacc.Bacc("TRN2", target_bir_lowering=False, num_devices=1, dynamic_dma_scratch_size=1024)
    arrays = {name: np.ascontiguousarray(inputs[name]) for name in INPUTS}
    ins = [nc.dram_tensor(name, a.shape, mybir.dt.from_np(a.dtype), kind="ExternalInput").ap() for name, a in arrays.items()]
    outs = [nc.dram_tensor(name, shape, F32, kind="ExternalOutput").ap() for name, shape in OUTPUTS]
    build(nc, ins, outs)
    results = run_bass_kernel_spmd(nc, [arrays], core_ids=[0]).results[0]
    return tuple(results[name] for name, _ in OUTPUTS)
```

```python
from contextlib import ExitStack

import numpy as np

import concourse.bass as bass
from concourse import mybir

F32 = mybir.dt.float32
F32R = mybir.dt.float32r
ALU = mybir.AluOpType
ACT = mybir.ActivationFunctionType
AX = mybir.AxisListType

P = 128
D = 1024
KB = D // P
L = 2048
NS = 8
T = L + NS
NH, DQK, DHV = 4, 128, 256
NCH = L // P
HC = NCH * NH
CW = 3
EPS = 1e-6
NEG = -1e30
BIG = 3e38
COL = dict(q=0, k=512, v=1024, o=2056, z=3080, b=4104, c=5128, x=6152, s=7176, gm=8200, gc=9224)
VW = D + 2 * NH
VC = VW // 3
NT = L // P + 1
TILES = [(0, 412), (412, 412), (824, 412), (1236, 410), (1646, 410)]
NTILE = len(TILES)
TN = 294
NTC = 7
TP = TN * NTC
QSCALE = DQK ** -0.5


class Chain:

    def __init__(self, eng, sem):
        self.eng, self.sem, self.base, self.n = eng, sem, 0, 0

    def link(self, ins):
        ins.then_inc(self.sem, 1)
        self.n += 1
        self.eng.wait_ge(self.sem, self.base + self.n)

    def enter(self, i, per):
        self.saved, self.per = self.base + self.n, per
        self.base, self.n = self.saved + i * per, 0

    def leave(self, rounds):
        assert self.n == self.per, (self.n, self.per)
        self.base, self.n = self.saved + rounds * self.per, 0


def sbuf(nc, ctx, name, shape, dt=F32):
    return ctx.enter_context(nc.sbuf_tensor(name, shape, dt))


def psum(nc, ctx, name, shape):
    return ctx.enter_context(nc.psum_tensor(name, shape, F32))


class Shared:
    pass


def build(nc, inputs, outputs):
    def dram(name, *shape):
        return nc.dram_tensor(name, shape, F32, kind="Internal").ap()

    top, early = ExitStack(), ExitStack()
    with top:
        top.enter_context(nc.allow_non_contiguous_dma(reason="small per-channel columns"))
        RH = sbuf(nc, top, "RH", [P, KB, T], F32R)
        RL = sbuf(nc, top, "RL", [P, KB, T], F32R)
        g = Shared()
        (g.x_prompt, g.x_sample, g.state_C, g.state_n, g.state_m, g.state_conv, g.norm_w, g.w_in, g.b_i, g.b_f,
         g.head_norm_w, g.conv_w, g.w_proj_m, g.w_proj_c, g.w_out, g.final_norm_w) = inputs
        (g.y_prompt, g.y_sample, g.C_prompt, g.n_prompt, g.m_prompt, g.conv_prompt,
         g.C_sample, g.n_sample, g.m_sample, g.conv_sample) = outputs
        g.v_rows = dram("v_rows", T, D)
        g.qT_d = dram("qT_d", NH, P, TP)
        g.kT_d = dram("kT_d", NH, P, TP)
        g.gate_d = dram("gate_d", KB, P, TP)
        g.hg_d = dram("hg_d", KB, P, TP)
        g.cv_d = dram("cv_d", KB, P, TP)
        g.tm_d = dram("tm_d", KB, P, TP)
        g.tc_d = dram("tc_d", KB, P, TP)
        g.mix_d = dram("mix_d", KB, P, TP)
        g.negM_d = dram("negM_d", NCH, NH, P)
        g.qk_rows = dram("qk_rows", NS, 2 * NH * DQK)
        g.fir_d = dram("fir_d", 3, NS * NH)
        g.RH, g.RL, g.RHf = RH, RL, RH[:, :, :].bitcast(F32)
        g.ident = sbuf(nc, top, "ident", [P, P])
        g.S = sbuf(nc, top, "stages", [P, 2, VW])
        g.stage_in = {name: [top.enter_context(nc.semaphore(f"{name}_in{j}")) for j in range(2)] for name in ("wb", "wc", "mix")}
        g.mix_out = top.enter_context(nc.semaphore("mix_out"))
        g.IF = sbuf(nc, early, "IF", [P, NT, 2 * NH])
        with early:
            phase_a(nc, g)
            phase_b(nc, g)
        phase_c(nc, g)
        phase_d(nc, g)


def phase_a(nc, g):
    ctx = ExitStack()
    sem = lambda n: ctx.enter_context(nc.semaphore("a_" + n))
    NSTG = 4
    WH = sbuf(nc, ctx, "wv_hi", [P, KB, VW], F32R)
    WL = sbuf(nc, ctx, "wv_lo", [P, KB, VW], F32R)
    xt = [sbuf(nc, ctx, f"xt{j}", [P, D]) for j in range(2)]
    stage = [sbuf(nc, ctx, f"wv_stage{j}", [P, VW]) for j in range(2)] + [g.S[:, 1], g.S[:, 0]]
    v_out, junk = stage[0:2], stage[2]
    nw = sbuf(nc, ctx, "nw", [P, D])
    stat = sbuf(nc, ctx, "stat", [P, 3, 2])
    half = sbuf(nc, ctx, "half", [P, 1])
    TR = [psum(nc, ctx, f"a_tr{j}", [P, 4, P]) for j in range(2)]
    V = [psum(nc, ctx, f"a_v{j}", [P, 512]) for j in range(6)]

    x_in = [sem("x_in0"), sem("x_in1")]
    wv_in = [sem(f"wv_in{j}") for j in range(NSTG)]
    const_in, const_set = sem("const_in"), sem("const_set")
    wv_hi, wv_lo = sem("wv_hi"), sem("wv_lo")
    squared, var_set, rstd_set, normed = sem("squared"), sem("var_set"), sem("rstd_set"), sem("normed")
    transposed, hi_set, lo_set = sem("transposed"), sem("hi_set"), sem("lo_set")
    v_done, v_act, v_dve = sem("v_done"), sem("v_act"), sem("v_dve")
    v_stored = [sem("v_stored0"), sem("v_stored1")]

    def rows(i):
        return NS if isinstance(i, int) and i == NT - 1 else P

    def at(i):
        return slice(i * P, i * P + rows(i)) if isinstance(i, int) else bass.ds(i * P, P)

    def turned(i):
        return [V[j][:, :].rearrange("p (a b) -> p a b", a=4) for j in (4, 5)] if isinstance(i, int) and i == 1 else TR

    def seen(i, par):
        return 8 * i + (8 if par else 16)

    xp = g.x_prompt[0].rearrange("(t p) d -> t p d", p=P)
    w_v = g.w_in[0].rearrange("(k p) n -> k p n", p=P)

    def over_tiles(eng, body):
        body(2, 0)
        with eng.Fori(0, 6) as j:
            body(2 * j + 3, 1)
            body(2 * j + 4, 0)
        body(NT - 2, 1)
        body(NT - 1, 0)

    with nc.Block() as block:

        @block.sync
        def _(sp):
            def load_w(k):
                sp.dma_start(stage[k % NSTG][:, :], w_v[k, :, COL["v"]:COL["v"] + VW]).then_inc(wv_in[k % NSTG], 16)

            def load_x(i, par):
                src = g.x_sample[:, 0, :] if rows(i) == NS else (xp[i] if isinstance(i, int) else xp[bass.ds(i, 1)].rearrange("a p d -> (a p) d"))
                sp.dma_start(xt[par][:rows(i), :], src).then_inc(x_in[par], 16)

            def store(i, par):
                sp.wait_ge(v_act, i + 1)
                sp.wait_ge(v_dve, i + 1)
                sp.dma_start(g.v_rows[at(i), :], v_out[par][:rows(i), 0:D]).then_inc(v_stored[par], 16)

            load_x(0, 0)
            sp.dma_start(nw[:, :], g.norm_w[0].partition_broadcast(P)).then_inc(const_in, 16)
            load_x(1, 1)
            load_w(0)
            for k in range(1, KB):
                if k >= NSTG:
                    sp.wait_ge(wv_lo, k - NSTG + 1)
                load_w(k)
            sp.wait_ge(transposed, 1)
            load_x(2, 0)

            def body(i, par):
                if rows(i) == P:
                    sp.wait_ge(transposed, i)
                    load_x(i + 1, 1 - par)
                if isinstance(i, int) and i == 2:
                    store(0, 0)
                store(i - 1, 1 - par)

            over_tiles(sp, body)
            for j, name in enumerate(("q", "k")):
                if j == 1:
                    sp.wait_ge(squared, NT)
                sp.dma_start(g.S[:, j, 0:D].rearrange("p (k n) -> p k n", k=KB),
                             g.w_in[0].rearrange("(k p) n -> p k n", p=P)[:, :, COL[name]:COL[name] + P]).then_inc(g.stage_in["wb"][j], 16)
            store(NT - 1, 0)
            sp.wait_ge(v_stored[0], seen(NT - 1, 0))
            sp.wait_ge(v_stored[1], seen(NT - 2, 1))

        @block.gpsimd
        def _(pool):
            nc.gpsimd.memset(half[:, :], -0.5).then_inc(const_set, 1)
            nc.gpsimd.memset(g.ident[:, :], 0.0).then_inc(const_set, 1)
            pool.wait_ge(const_set, 2)
            nc.gpsimd.affine_select(out=g.ident[:, :], in_=g.ident[:, :], compare_op=ALU.not_equal, fill=1.0,
                                    base=0, pattern=[[-1, P]], channel_multiplier=1).then_inc(const_set, 1)

            def rstd(i, par):
                n = rows(i)
                pool.wait_ge(var_set, i + 1)
                nc.gpsimd.tensor_tensor(stat[:n, 2, par:par + 1], stat[:n, 1, par:par + 1], half[:n, :],
                                        ALU.pow).then_inc(rstd_set, 1)

            rstd(0, 0)
            rstd(1, 1)
            over_tiles(pool, rstd)

        @block.scalar
        def _(act):
            def square(i, par):
                n = rows(i)
                act.wait_ge(x_in[par], seen(i, par))
                if isinstance(i, int) and i < 2:
                    rubbish = WL[:n, KB - 1 - i, 0:D]
                else:
                    act.wait_ge(wv_lo, KB)
                    act.wait_ge(squared, i)
                    rubbish = junk[:n, 0:D]
                nc.scalar.activation(rubbish, xt[par][:n, :], ACT.Square,
                                     accum_out=stat[:n, 0, par:par + 1]).then_inc(squared, 1)

            def hi(i):
                act.wait_ge(transposed, i + 1)
                for j in range(2):
                    nc.scalar.activation(g.RH[:, 4 * j:4 * j + 4, at(i)], turned(i)[j][:, :, 0:rows(i)], ACT.Copy).then_inc(hi_set, 1)

            def split(k):
                act.wait_ge(wv_in[k % NSTG], 16 * (k // NSTG + 1))
                nc.scalar.activation(WH[:, k, :], stage[k % NSTG][:, :], ACT.Copy).then_inc(wv_hi, 1)

            def evac(i, par):
                n = rows(i)
                act.wait_ge(v_done, i + 1)
                if not isinstance(i, int) or i >= 2:
                    act.wait_ge(v_stored[par], seen(i, par) - 16)
                nc.scalar.activation(v_out[par][:n, VC:2 * VC], V[3 * par + 1][:n, 0:VC], ACT.Copy).then_inc(v_act, 1)

            square(0, 0)
            square(1, 1)
            split(0)
            hi(0)
            hi(1)
            for k in range(1, KB):
                split(k)
            square(2, 0)

            def body(i, par):
                hi(i)
                if rows(i) == P:
                    square(i + 1, 1 - par)
                if isinstance(i, int) and i == 2:
                    evac(0, 0)
                evac(i - 1, 1 - par)

            over_tiles(act, body)
            evac(NT - 1, 0)

        @block.vector
        def _(dve):
            def norm(i, par):
                n = rows(i)
                dve.wait_ge(squared, i + 1)
                nc.vector.tensor_scalar(stat[:n, 1, par:par + 1], stat[:n, 0, par:par + 1], 1.0 / D, EPS,
                                        ALU.mult, ALU.add).then_inc(var_set, 1)
                if isinstance(i, int) and i == 0:
                    dve.wait_ge(const_in, 16)
                dve.wait_ge(rstd_set, i + 1)
                nc.vector.scalar_tensor_tensor(out=xt[par][:n, :], in0=xt[par][:n, :], scalar=stat[:n, 2, par:par + 1],
                                               in1=nw[:n, :], op0=ALU.mult, op1=ALU.mult).then_inc(normed, 1)

            def lo(i):
                for j in range(2):
                    dve.wait_ge(hi_set, 2 * i + j + 1)
                    nc.vector.tensor_tensor(g.RL[:, 4 * j:4 * j + 4, at(i)], turned(i)[j][:, :, 0:rows(i)],
                                            g.RHf[:, 4 * j:4 * j + 4, at(i)], ALU.subtract).then_inc(lo_set, 1)

            def split(k):
                dve.wait_ge(wv_hi, k + 1)
                nc.vector.tensor_tensor(WL[:, k, :], stage[k % NSTG][:, :], WH[:, k, :].bitcast(F32),
                                        ALU.subtract).then_inc(wv_lo, 1)

            def evac(i, par):
                n = rows(i)
                dve.wait_ge(v_done, i + 1)
                if not isinstance(i, int) or i >= 2:
                    dve.wait_ge(v_stored[par], seen(i, par) - 16)
                nc.vector.tensor_copy(v_out[par][:n, 0:VC], V[3 * par][:n, 0:VC])
                gates = g.IF[:n, i, :] if isinstance(i, int) else g.IF[:n, bass.ds(i, 1), :].rearrange("p a n -> p (a n)")
                nc.vector.tensor_copy(gates, V[3 * par + 2][:n, D - 2 * VC:VC])
                nc.vector.tensor_copy(v_out[par][:n, 2 * VC:D], V[3 * par + 2][:n, 0:D - 2 * VC]).then_inc(v_dve, 1)

            norm(0, 0)
            norm(1, 1)
            lo(0)
            lo(1)
            split(0)
            for k in range(1, KB):
                split(k)
            norm(2, 0)

            def body(i, par):
                lo(i)
                if rows(i) == P:
                    norm(i + 1, 1 - par)
                if isinstance(i, int) and i == 2:
                    evac(0, 0)
                evac(i - 1, 1 - par)

            over_tiles(dve, body)
            evac(NT - 1, 0)

        @block.tensor
        def _(pe):
            def transpose(i):
                n = rows(i)
                pe.wait_ge(normed, i + 1)
                if i > 1:
                    pe.wait_ge(lo_set, 2 * i)
                for k in range(KB):
                    last = nc.tensor.transpose(turned(i)[k // 4][:, k % 4, 0:n], xt[i % 2][:n, k * P:(k + 1) * P],
                                               g.ident[:n, :n])
                last.then_inc(transposed, 1)

            def block_product(i, j, k):
                n = rows(i)
                for m, (x, w) in enumerate(((g.RH, WH), (g.RH, WL), (g.RL, WH))):
                    last = nc.tensor.matmul(V[3 * (i % 2) + j][:n, 0:VC], x[:, k, i * P:i * P + n],
                                            w[:, k, j * VC:(j + 1) * VC], start=(k == 0 and m == 0), stop=(k == KB - 1 and m == 2))
                return last

            pe.wait_ge(const_set, 3)
            transpose(0)
            transpose(1)
            pe.wait_ge(lo_set, 4)
            for k in range(KB):
                pe.wait_ge(wv_lo, k + 1)
                if k == KB - 3:
                    transpose(2)
                for i in range(2):
                    for j in range(3):
                        last = block_product(i, j, k)
            last.then_inc(v_done, 2)
            for i in range(2, NT):
                if i + 1 < NT:
                    transpose(i + 1)
                pe.wait_ge(lo_set, 2 * i + 2)
                pe.wait_ge(v_act, i - 1)
                pe.wait_ge(v_dve, i - 1)
                for j in range(3):
                    for k in range(KB):
                        last = block_product(i, j, k)
                last.then_inc(v_done, 1)

    ctx.close()


def phase_b(nc, g):
    ctx = ExitStack()
    sem = lambda n: ctx.enter_context(nc.semaphore("b_" + n))
    WS = g.S[:, :, 0:D].rearrange("p a (k n) -> p a k n", k=KB)
    WH = sbuf(nc, ctx, "w_hi", [P, 2, KB, P], F32R)
    WL = sbuf(nc, ctx, "w_lo", [P, 2, KB, P], F32R)
    E0 = sbuf(nc, ctx, "row0", [P, TP])
    E1 = sbuf(nc, ctx, "row1", [P, TP])
    ZT = sbuf(nc, ctx, "z_tanh", [P, 2, 412])
    CV = sbuf(nc, ctx, "conv_tile", [P, 412])
    kT = sbuf(nc, ctx, "kT", [P, NH, P])
    qT = sbuf(nc, ctx, "qT", [P, NH, P])
    va = sbuf(nc, ctx, "v_ones", [P, NH, DHV + 1])
    nM = sbuf(nc, ctx, "negM", [P, NH, P])
    Dm = sbuf(nc, ctx, "decay", [P, NH, P])
    QW = sbuf(nc, ctx, "q_weighted", [P, NH, P])
    PT_ = sbuf(nc, ctx, "scores", [P, NH, P])
    KW = sbuf(nc, ctx, "k_weighted", [P, NH, P])
    HB = sbuf(nc, ctx, "h", [P, NH, DHV])
    GT = sbuf(nc, ctx, "gate", [P, KB, P])
    CS = sbuf(nc, ctx, "C_state", [P, NH, DHV + 1])
    mask = sbuf(nc, ctx, "mask", [P, P])
    cumU = sbuf(nc, ctx, "cum_upper", [P, P])
    ones = sbuf(nc, ctx, "ones", [P, P])
    half = sbuf(nc, ctx, "minus_half", [P, HC])
    bif = sbuf(nc, ctx, "b_if", [P, 2 * NH])
    hnw = sbuf(nc, ctx, "head_norm_q", [P, KB])
    cw = sbuf(nc, ctx, "conv_w_half", [P, CW, KB])
    cs = sbuf(nc, ctx, "conv_state", [P, KB, 2 * NS])
    csr = PT_[:2 * NS, :, :].rearrange("p a b -> p (a b)")
    csr2 = KW[:2 * NS, :, :].rearrange("p a b -> p (a b)")
    names = ("f_log", "f_abs", "b_cum", "a_in", "exp_negm", "w_end", "f_end", "m_prev")
    tk = {n: sbuf(nc, ctx, n, [P, HC]) for n in names}
    aT = GT[:HC, 0, :]
    cM = GT[:HC, 1, :]
    rowA = sbuf(nc, ctx, "row_A", [1, 4, HC + NH])
    col = sbuf(nc, ctx, "m_prev_col", [HC, 1])
    ss = sbuf(nc, ctx, "sumsq", [P, 3, NH])
    den = sbuf(nc, ctx, "den", [P, 2, 2])
    sm = sbuf(nc, ctx, "sample_small", [NS, 12, NH])
    dec = sbuf(nc, ctx, "sample_wide", [P, 8, 2 * NS * NH])
    G = [psum(nc, ctx, f"b_g{j}", [P, 512]) for j in range(2)]
    PS = psum(nc, ctx, "b_s", [P, NH, P])
    PT = [psum(nc, ctx, f"b_t{j}", [P, NH, P]) for j in range(2)]
    PN = [psum(nc, ctx, f"b_n{j}", [P, 512]) for j in range(2)]
    PC = psum(nc, ctx, "b_c", [P, 512])

    w_in_v = g.w_in[0].rearrange("(k p) n -> p k n", p=P)

    w_in_s = g.stage_in["wb"]
    w_hi, w_ready = sem("w_hi"), sem("w_ready")
    done = sem("tile_done")
    free = [sem("bank_free0"), sem("bank_free1")]
    z_set = sem("z_set")
    gate_set, u_used = sem("gate_set"), sem("u_used")
    row_out = [sem("row_out0"), sem("row_out1")]
    conv_out, state_out, misc_out = sem("conv_out"), sem("state_out"), sem("misc_out")
    const_in, const_set, pads = sem("const_in"), sem("const_set"), sem("pads")
    kq_in, v_in, gate_in, hg_out = sem("kq_in"), sem("v_in"), sem("gate_in"), sem("hg_out")
    s_done, kt_done, num_done, cu_done, ht_done = (sem(n) for n in ("s_done", "kt_done", "num_done", "cu_done", "ht_done"))
    dpre, kw_set, qw_set, p_set = sem("dpre"), sem("kw_set"), sem("qw_set"), sem("p_set")
    wint_set, dexp_set, sq_set = sem("wint_set"), sem("dexp_set"), sem("sq_set")
    h_set, c_set, var_set, rs_set, hn_set, hg_set = (sem(n) for n in ("h_set", "c_set", "var_set", "rs_set", "hn_set", "hg_set"))
    biased, act_own, softplus, lf_set, b_mm, a_set, a_mm, cm_set, al_mm, m_set, m_mm, M_set, mt_mm, exps_in, exps_set = (
        sem(n) for n in ("biased", "act_own", "softplus", "lf_set", "b_mm", "a_set", "a_mm", "cm_set", "al_mm", "m_set",
                         "m_mm", "M_set", "mt_mm", "exps_in", "exps_set"))
    dve_own = sem("dve_own")
    ct_mm, ct_set, c_out = sem("ct_mm"), sem("ct_set"), sem("c_out")
    dec_in, dec_mm, dec_rows, dec_out, dec_bc = (sem(n) for n in ("dec_in", "dec_mm", "dec_rows", "dec_out", "dec_bc"))
    dec_kq_in, dec_c_in, dec_upd = sem("dec_kq_in"), sem("dec_c_in"), sem("dec_upd")
    dec_sq, dec_sum, dec_var, dec_rs, dec_h = (sem(n) for n in ("dec_sq", "dec_sum", "dec_var", "dec_rs", "dec_h"))

    from_one = dict(sp=(row_out[0], row_out[1], conv_out), act=(sq_set,), dve=(gate_set, p_set, hg_set, dec_upd),
                    pe=(done, num_done, cu_done, ht_done))

    def sl(i, n=1):
        return slice(i * n, i * n + n) if isinstance(i, int) else bass.ds(i * n, n)

    NP1, NP2, NP3, NP4 = 4, 8, 16, 8
    F1, F2, F3, F4 = 0, NP1, NP1 + NP2, NP1 + NP2 + NP3
    NPAIR = F4 + NP4

    def block_waits(eng, pair, par):
        eng.wait_ge(free[par], NTILE * pair + (NTILE if par else 3) + 1)

    def bc(ap, n):
        return ap.unsqueeze(2).to_broadcast([ap.shape[0], ap.shape[1], n])

    row_q, row_k, row_gate, row_conv, row_tm, row_tc = 0, 0, NP1, NP1 + NP2, NP1, NP1 + NP2 + KB

    with nc.Block() as block:

        @block.sync
        def _(sp):
            for s in from_one["sp"]:
                sp.sem_inc(s, 1)

            def load_w(m_par, pair, c0):
                sp.wait_ge(w_ready, 2 * pair + m_par - 1)
                sp.dma_start(WS[:, m_par], w_in_v[:, :, bass.ds(c0, P)]).then_inc(w_in_s[m_par], 16)

            sp.dma_start(bif[:, 0:NH], g.b_i[0].partition_broadcast(P)).then_inc(const_in, 16)
            sp.dma_start(bif[:, NH:], g.b_f[0].partition_broadcast(P)).then_inc(const_in, 16)
            sp.dma_start(hnw[:, :], g.head_norm_w[0].rearrange("(k p) -> p k", p=P)).then_inc(const_in, 16)
            for j in range(CW):
                sp.dma_start(cw[:, j, :], g.conv_w[0, j].rearrange("(k p) -> p k", p=P)).then_inc(const_in, 16)
            state = g.state_conv[0].rearrange("b r d -> (b r) d")
            sp.dma_start(csr, state[:, 0:512]).then_inc(const_in, 16)
            sp.dma_start(csr2, state[:, 512:D]).then_inc(const_in, 16)
            sp.dma_start(sm[:, 0, :], g.state_m[0]).then_inc(const_in, 16)
            sp.dma_start(g.conv_sample[0, :, 0, :], g.state_conv[0, :, 1, :]).then_inc(state_out, 16)
            sp.wait_ge(const_set, 1)
            for a in (g.hg_d, g.cv_d, g.tm_d, g.tc_d):
                sp.dma_start(a[:, :, T:TP].rearrange("k p n -> p k n"),
                             dec[:, 0, 0:2 * KB].rearrange("p (k n) -> p k n", k=KB)).then_inc(pads, 16)
            load_w(0, 1, COL["q"] + P)
            load_w(1, 1, COL["k"] + P)
            sp.wait_ge(M_set, 1)
            sp.dma_start(g.negM_d.rearrange("c h t -> (c h) t"), aT).then_inc(misc_out, 16)
            sp.dma_start(g.m_prompt[0], rowA[0:1, 2, HC:HC + NH]).then_inc(misc_out, 16)
            sp.dma_start(g.m_sample[0], sm[:, 3, :]).then_inc(misc_out, 16)

            def one(a, i):
                return a[i] if isinstance(i, int) else a[bass.ds(i, 1)].rearrange("a p n -> (a p) n")

            def qk(h, last=False):
                pair = F1 + h
                if not (isinstance(h, int) and h == 0):
                    load_w(0, pair + 1, COL["o"] if last else COL["q"] + (h + 1) * P)
                    load_w(1, pair + 1, COL["z"] if last else COL["k"] + (h + 1) * P)
                block_waits(sp, pair, 0)
                sp.dma_start(one(g.qT_d, h)[:, 0:T], E0[:, 0:T]).then_inc(row_out[0], 16)
                block_waits(sp, pair, 1)
                sp.dma_start(one(g.kT_d, h)[:, 0:T], E1[:, 0:T]).then_inc(row_out[1], 16)

            qk(0)
            with sp.Fori(1, NP1 - 1) as h:
                qk(h)
            qk(NP1 - 1, True)

            def load_kq(c):
                if not (isinstance(c, int) and c == 0):
                    sp.wait_ge(p_set, 1 + c)
                at = sl(c, P)
                sp.dma_start(kT[:, :, :], g.kT_d[:, :, at].rearrange("h p t -> p h t")).then_inc(kq_in, 16)
                sp.dma_start(qT[:, :, :], g.qT_d[:, :, at].rearrange("h p t -> p h t")).then_inc(kq_in, 16)
                sp.dma_start(nM[:, :, :], (g.negM_d[c] if isinstance(c, int) else g.negM_d[bass.ds(c, 1)].rearrange("a h t -> (a h) t")).partition_broadcast(P)).then_inc(kq_in, 16)

            def load_v(c):
                if not (isinstance(c, int) and c == 0):
                    sp.wait_ge(cu_done, 1 + NH * c)
                sp.dma_start(va[:, :, 0:DHV], g.v_rows[sl(c, P), :].rearrange("t (h v) -> t h v", h=NH)).then_inc(v_in, 16)

            def load_gate(c):
                if not (isinstance(c, int) and c == 0):
                    sp.wait_ge(hg_out, 16 * c)
                sp.dma_start(GT[:, :, :], g.gate_d[:, :, sl(c, P)].rearrange("k p t -> p k t")).then_inc(gate_in, 16)

            def store_hg(c):
                sp.wait_ge(hg_set, 1 + c + 1)
                sp.dma_start(g.hg_d[:, :, sl(c, P)].rearrange("k p t -> p k t"), GT[:, :, :]).then_inc(hg_out, 16)

            def oz(i, last=False):
                pair = F2 + i
                load_w(0, pair + 1, COL["c"] if last else COL["o"] + (i + 1) * P)
                load_w(1, pair + 1, COL["x"] if last else COL["z"] + (i + 1) * P)
                sp.wait_ge(gate_set, 1 + i + 1)
                sp.dma_start(one(g.gate_d, i)[:, 0:T], E1[:, 0:T]).then_inc(row_out[1], 16)

            sp.wait_ge(row_out[0], 1 + 16 * NP1)
            sp.wait_ge(row_out[1], 1 + 16 * NP1)
            sp.wait_ge(misc_out, 48)
            load_kq(0)
            load_v(0)
            with sp.Fori(0, NP2 - 1) as i:
                oz(i)
            oz(NP2 - 1, True)

            sp.wait_ge(row_out[1], 1 + 16 * (NP1 + NP2))
            load_gate(0)

            def conv(i, last=False):
                pair = F3 + 2 * i
                c = 2 * i
                load_w(0, pair + 1, COL["s"] + i * P)
                load_kq(c + 1)
                load_w(1, pair + 1, COL["b"] + i * P)
                load_v(c + 1)
                store_hg(c)
                load_gate(c + 1)
                block_waits(sp, pair, 1)
                sp.dma_start(g.conv_sample[0, :, 1, sl(i, P)].rearrange("b d -> d b"), E0[:, L + 2:L + 2 + NS]).then_inc(conv_out, 16)
                sp.dma_start(g.conv_prompt[0, 0][:, sl(i, P)].rearrange("r d -> d r"), E0[:, L:L + 2]).then_inc(conv_out, 16)
                load_w(0, pair + 2, COL["gm"] if last else COL["c"] + (i + 1) * P)
                if not last:
                    load_kq(c + 2)
                load_w(1, pair + 2, COL["gc"] if last else COL["x"] + (i + 1) * P)
                if not last:
                    load_v(c + 2)
                store_hg(c + 1)
                if not last:
                    load_gate(c + 2)
                block_waits(sp, pair + 1, 1)
                sp.dma_start(one(g.cv_d, i)[:, 0:T], E1[:, 0:T]).then_inc(row_out[1], 16)

            with sp.Fori(0, KB - 1) as i:
                conv(i)
            conv(KB - 1, True)

            sp.wait_ge(hg_out, 16 * NCH)
            sp.dma_start(GT[:, 0, 0:NH * NS].rearrange("p (h b) -> p h b", h=NH),
                         g.qT_d[:, :, L:T].rearrange("h p b -> p h b")).then_inc(dec_in, 16)
            sp.dma_start(GT[:, 0, NH * NS:2 * NH * NS].rearrange("p (h b) -> p h b", h=NH),
                         g.kT_d[:, :, L:T].rearrange("h p b -> p h b")).then_inc(dec_in, 16)
            sp.dma_start(dec[:, 7, :].rearrange("p (k b) -> p k b", k=KB),
                         g.gate_d[:, :, L:T].rearrange("k p b -> p k b")).then_inc(dec_in, 16)
            sp.dma_start(QW[:NS, :, :], g.state_n[0]).then_inc(dec_in, 16)
            sp.dma_start(va[:NS, 0:NH, 0:DHV], g.v_rows[L:T, :].rearrange("t (h v) -> t h v", h=NH)).then_inc(dec_in, 16)
            def store_gates(i):
                block_waits(sp, F4 + i, 0)
                sp.dma_start(one(g.tm_d, i)[:, 0:T], E0[:, 0:T]).then_inc(row_out[0], 16)
                block_waits(sp, F4 + i, 1)
                sp.dma_start(one(g.tc_d, i)[:, 0:T], E1[:, 0:T]).then_inc(row_out[1], 16)

            load_w(0, F4 + 1, COL["gm"] + P)
            load_w(1, F4 + 1, COL["gc"] + P)
            sp.wait_ge(ct_set, 1)
            for h in range(NH):
                sp.dma_start(g.C_prompt[0, 0, h].rearrange("(a v) d -> v a d", v=P), HB[:, h, :].rearrange("p (a d) -> p a d", a=2)).then_inc(c_out, 16)
            sp.dma_start(g.n_prompt[0, 0].rearrange("h d -> d h"), CS[:, :, DHV]).then_inc(c_out, 16)
            store_gates(0)
            load_w(0, F4 + 2, COL["gm"] + 2 * P)
            sp.wait_ge(dec_rows, 1)
            sp.dma_start(g.qk_rows[:, 0:512], PT_[:NS, :, :].rearrange("p h d -> p (h d)")).then_inc(dec_out, 16)
            sp.dma_start(g.qk_rows[:, 512:1024], KW[:NS, :, :].rearrange("p h d -> p (h d)")).then_inc(dec_out, 16)
            sp.dma_start(g.n_sample[0], QW[:NS, :, :]).then_inc(dec_out, 16)
            for j in range(3):
                sp.dma_start(g.fir_d[j].rearrange("(b h) -> b h", h=NH), sm[:, 5 + j, :]).then_inc(dec_out, 16)
            sp.wait_ge(dec_out, 16 * 6)
            sp.wait_ge(pads, 64)
            sp.dma_start(dec[:, 0, :], g.fir_d[0:2].rearrange("j n -> (j n)").partition_broadcast(P)).then_inc(dec_bc, 16)
            sp.dma_start(dec[:, 1, 0:NS * NH], g.fir_d[2].partition_broadcast(P)).then_inc(dec_bc, 16)

            def load_sample(b):
                rows = g.qk_rows[b] if isinstance(b, int) else g.qk_rows[bass.ds(b, 1)].rearrange("a n -> (a n)")
                sp.wait_ge(dec_upd, 1 + b)
                sp.dma_start(qT[:, :, :].rearrange("p h d -> p (h d)"), rows[0:512].partition_broadcast(P)).then_inc(dec_kq_in, 16)
                sp.dma_start(kT[:, :, :].rearrange("p h d -> p (h d)"), rows[512:1024].partition_broadcast(P)).then_inc(dec_kq_in, 16)
                sp.wait_ge(state_out, 16 * (b + 1))
                src = g.state_C[0, b] if isinstance(b, int) else g.state_C[0, bass.ds(b, 1)].rearrange("a h v d -> (a h) v d")
                sp.dma_start(GT[:, :, :], src.rearrange("h (a v) d -> v (h a) d", v=P)).then_inc(dec_c_in, 16)

            def store_C(b):
                sp.wait_ge(dec_upd, 1 + b + 1)
                dst = g.C_sample[0, b] if isinstance(b, int) else g.C_sample[0, bass.ds(b, 1)].rearrange("a h v d -> (a h) v d")
                sp.dma_start(dst.rearrange("h (a v) d -> v (h a) d", v=P), GT[:, :, :]).then_inc(state_out, 16)

            load_sample(0)
            load_w(1, F4 + 2, COL["gc"] + 2 * P)
            store_C(0)

            def gates(i, last=False):
                load_sample(i)
                store_gates(i)
                if not last:
                    load_w(0, F4 + i + 2, COL["gm"] + (i + 2) * P)
                    load_w(1, F4 + i + 2, COL["gc"] + (i + 2) * P)
                store_C(i)

            with sp.Fori(1, NP4 - 2) as i:
                gates(i)
            gates(NP4 - 2, True)
            load_sample(NS - 1)
            for j in range(2):
                sp.wait_ge(w_ready, 2 * NPAIR - 1 + j)
                sp.dma_start(g.S[:, j, 0:D], g.w_proj_m[0, j * P:(j + 1) * P, :]).then_inc(g.stage_in["wc"][j], 16)
            store_C(NS - 1)
            sp.wait_ge(dec_h, 1)
            sp.dma_start(g.hg_d[:, :, L:T].rearrange("k p b -> p k b"),
                         dec[:, 6, :].rearrange("p (k b) -> p k b", k=KB)).then_inc(hg_out, 16)
            block_waits(sp, NPAIR - 1, 0)
            sp.dma_start(g.tm_d[NP4 - 1][:, 0:T], E0[:, 0:T]).then_inc(row_out[0], 16)
            cut = TILES[NTILE - 1][0]
            sp.wait_ge(free[0], NTILE * NPAIR + 1)
            sp.dma_start(g.tc_d[NP4 - 1][:, 0:cut], E1[:, 0:cut]).then_inc(row_out[1], 16)
            block_waits(sp, NPAIR - 1, 1)
            sp.dma_start(g.tc_d[NP4 - 1][:, cut:T], E1[:, cut:T]).then_inc(row_out[1], 16)
            sp.wait_ge(row_out[0], 1 + 16 * (NP1 + NP4))
            sp.wait_ge(row_out[1], 1 + 16 * (NP1 + NP2 + KB + NP4 + 1))
            sp.wait_ge(hg_out, 16 * (NCH + 1))
            sp.wait_ge(pads, 64)
            sp.wait_ge(c_out, 16 * 5)
            sp.wait_ge(state_out, 16 * 9)
            sp.wait_ge(conv_out, 1 + 32 * KB)
            sp.wait_ge(misc_out, 48)
            sp.wait_ge(dec_out, 96)

        @block.gpsimd
        def _(pool):
            nc.gpsimd.memset(dec[:, 0, 0:2 * KB], 0.0).then_inc(const_set, 1)
            nc.gpsimd.memset(half[:, :], -0.5)
            nc.gpsimd.memset(ones[:, :], 1.0).then_inc(const_set, 1)
            nc.gpsimd.memset(mask[:, :], BIG).then_inc(const_set, 1)
            nc.gpsimd.memset(va[:, :, DHV], 1.0).then_inc(const_set, 1)
            pool.wait_ge(const_set, 3)
            nc.gpsimd.affine_select(out=cumU[:, :], in_=ones[:, :], compare_op=ALU.is_ge, fill=0.0,
                                    base=0, pattern=[[1, P]], channel_multiplier=-1).then_inc(const_set, 1)
            nc.gpsimd.affine_select(out=mask[:, :], in_=mask[:, :], compare_op=ALU.is_ge, fill=NEG,
                                    base=0, pattern=[[1, P]], channel_multiplier=-1).then_inc(const_set, 1)
            with pool.Fori(0, NCH) as c:
                pool.wait_ge(var_set, c + 1)
                nc.gpsimd.tensor_tensor(ss[:, 2, :], ss[:, 1, :], half[:, 0:NH], ALU.pow).then_inc(rs_set, 1)
            pool.wait_ge(dec_var, 1)
            nc.gpsimd.tensor_tensor(dec[:, 4, 0:NS * NH], dec[:, 3, 0:NS * NH], half[:, 0:NS * NH], ALU.pow).then_inc(dec_rs, 1)

        @block.scalar
        def _(act):
            for s in from_one["act"]:
                act.sem_inc(s, 1)

            def split_hi(pair, par):
                act.wait_ge(w_in_s[par], 16 * (pair + 1))
                if not (isinstance(pair, int) and pair == 0):
                    act.wait_ge(done, 1 + NTILE * (2 * pair + par - 1))
                nc.scalar.activation(WH[:, par], WS[:, par], ACT.Copy).then_inc(w_hi, 1)

            split_hi(0, 0)
            fl, fa = tk["f_log"], tk["f_abs"]
            act.wait_ge(biased, 1)
            nc.scalar.activation(fa[:, :], fl[:, :], ACT.Abs)
            nc.scalar.activation(sm[:, 9, :], sm[:, 2, :], ACT.Abs).then_inc(act_own, 1)
            act.wait_ge(act_own, 1)
            nc.scalar.activation(fa[:, :], fa[:, :], ACT.Exp, scale=-1.0)
            nc.scalar.activation(sm[:, 9, :], sm[:, 9, :], ACT.Exp, scale=-1.0).then_inc(act_own, 1)
            act.wait_ge(act_own, 2)
            nc.scalar.activation(fa[:, :], fa[:, :], ACT.Ln, bias=1.0)
            nc.scalar.activation(sm[:, 9, :], sm[:, 9, :], ACT.Ln, bias=1.0).then_inc(softplus, 1)

            def tiles_of(pair, par):
                for t, (c0, n) in enumerate(TILES):
                    j = par * NTILE + t
                    act.wait_ge(done, 1 + 2 * NTILE * pair + j + 1)
                    yield t, j % 2, c0, n

            def tanh_z(pair, par, t):
                c0, n = TILES[t]
                b = (par * NTILE + t) % 2
                act.wait_ge(done, 1 + 2 * NTILE * pair + par * NTILE + t + 1)
                nc.scalar.activation(ZT[:, b, 0:n], G[b][:, 0:n], ACT.Tanh, scale=0.5).then_inc(z_set, 1)

            with act.Fori(0, NP1) as h:
                pair = F1 + h
                split_hi(pair, 1)
                act.wait_ge(row_out[0], 1 + 16 * h)
                for t, b, c0, n in tiles_of(pair, 0):
                    nc.scalar.activation(E0[:, c0:c0 + n], G[b][:, 0:n], ACT.Copy).then_inc(free[b], 1)
                split_hi(pair + 1, 0)
                act.wait_ge(row_out[1], 1 + 16 * h)
                for t, b, c0, n in tiles_of(pair, 1):
                    nc.scalar.activation(E1[:, c0:c0 + n], G[b][:, 0:n], ACT.Copy, scale=QSCALE).then_inc(free[b], 1)

            act.wait_ge(exps_in, 1)
            nc.scalar.activation(tk["exp_negm"][:, :], tk["exp_negm"][:, :], ACT.Exp, scale=-1.0)
            nc.scalar.activation(tk["w_end"][:, :], tk["w_end"][:, :], ACT.Exp)
            nc.scalar.activation(tk["f_end"][:, :], tk["f_end"][:, :], ACT.Exp)
            nc.scalar.activation(sm[:, 4, :], sm[:, 3, :], ACT.Exp, scale=-1.0)
            nc.scalar.activation(sm[:, 5:7, :], sm[:, 5:7, :], ACT.Exp).then_inc(exps_set, 1)
            act.wait_ge(row_out[0], 1 + 16 * NP1)
            with act.Fori(0, NP2) as i:
                pair = F2 + i
                split_hi(pair, 1)
                act.wait_ge(gate_set, 1 + i)
                for t, b, c0, n in tiles_of(pair, 0):
                    nc.scalar.activation(E0[:, c0:c0 + n], G[b][:, 0:n], ACT.Tanh, scale=0.5).then_inc(free[b], 1)
                split_hi(pair + 1, 0)
                for t in range(NTILE):
                    tanh_z(pair, 1, t)

            def chunk_act(c, s):
                if s == 0:
                    act.wait_ge(kq_in, 48 * (c + 1))
                    act.wait_ge(num_done, 1 + NH * c)
                    for h in range(NH):
                        last = nc.scalar.activation(QW[:, h, :], nM[:, h, :], ACT.Exp, bias=tk["m_prev"][:, bass.ds(NH * c + h, 1)])
                    last.then_inc(wint_set, 1)
                    act.wait_ge(dpre, c + 1)
                    for h in range(NH):
                        last = nc.scalar.activation(Dm[:, h, :], Dm[:, h, :], ACT.Exp, bias=tk["a_in"][:, bass.ds(NH * c + h, 1)])
                    last.then_inc(dexp_set, 1)
                elif 2 <= s < 2 + NH:
                    h = s - 2
                    act.wait_ge(sq_set, 1 + NH * c + h)
                    act.wait_ge(h_set, NH * c + h + 3)
                    nc.scalar.activation(Dm[:, 0:2, :].rearrange("p a b -> p (a b)"), HB[:, h, :], ACT.Square,
                                         accum_out=ss[:, 0, h:h + 1]).then_inc(sq_set, 1)

            with act.Fori(0, KB) as i:
                pair = F3 + 2 * i
                split_hi(pair, 1)
                act.wait_ge(u_used, i + 1)
                act.wait_ge(conv_out, 1 + 32 * i)
                for s in range(NTILE):
                    chunk_act(2 * i, s)
                    c0, n = TILES[s]
                    act.wait_ge(done, 1 + 2 * NTILE * pair + s + 1)
                    nc.scalar.activation(E0[:, 2 + c0:2 + c0 + n], G[s % 2][:, 0:n], ACT.Copy).then_inc(free[s % 2], 1)
                split_hi(pair + 1, 0)
                for s in range(NTILE):
                    chunk_act(2 * i, NTILE + s)
                split_hi(pair + 1, 1)
                for s in range(NTILE):
                    chunk_act(2 * i + 1, s)
                    tanh_z(pair + 1, 0, s)
                split_hi(pair + 2, 0)
                for s in range(NTILE):
                    chunk_act(2 * i + 1, NTILE + s)

            def gate_rows(i, last=False):
                pair = F4 + i
                split_hi(pair, 1)
                act.wait_ge(row_out[0], 1 + 16 * (row_tm + i))
                for t, b, c0, n in tiles_of(pair, 0):
                    nc.scalar.activation(E0[:, c0:c0 + n], G[b][:, 0:n], ACT.Tanh, scale=0.5).then_inc(free[b], 1)
                if not last:
                    split_hi(pair + 1, 0)
                act.wait_ge(row_out[1], 1 + 16 * (row_tc + i))
                for t, b, c0, n in tiles_of(pair, 1):
                    nc.scalar.activation(E1[:, c0:c0 + n], G[b][:, 0:n], ACT.Tanh, scale=0.5).then_inc(free[b], 1)

            act.wait_ge(u_used, KB + 1)
            act.wait_ge(conv_out, 1 + 32 * KB)
            with act.Fori(0, NP4 - 1) as i:
                gate_rows(i)
            gate_rows(NP4 - 1, True)

        @block.vector
        def _(dve):
            for s in from_one["dve"]:
                dve.sem_inc(s, 1)

            own = Chain(dve, dve_own)
            link = own.link

            def split_lo(pair, par):
                dve.wait_ge(w_hi, 2 * pair + par + 1)
                nc.vector.tensor_tensor(WL[:, par], WS[:, par], WH[:, par].bitcast(F32), ALU.subtract).then_inc(w_ready, 1)

            nc.vector.memset(ss[:, :, :], 0.0).then_inc(free[0], 1)
            nc.vector.memset(den[:, :, :], 0.0).then_inc(free[1], 1)
            nc.vector.memset(rowA[:, :, :], 0.0).then_inc(h_set, 2)
            split_lo(0, 0)
            nc.vector.memset(CS[:, :, :], 0.0).then_inc(c_set, NH)
            dve.wait_ge(const_in, 144)
            f3 = tk["f_log"][:, :].rearrange("p (c h) -> p c h", h=NH)
            a3 = tk["a_in"][:, :].rearrange("p (c h) -> p c h", h=NH)
            bi = bif[:, 0:NH].unsqueeze(1).to_broadcast([P, NCH, NH])
            bf = bif[:, NH:2 * NH].unsqueeze(1).to_broadcast([P, NCH, NH])
            nc.vector.tensor_tensor(a3, g.IF[:, 0:NCH, 0:NH], bi, ALU.add)
            nc.vector.tensor_tensor(f3, g.IF[:, 0:NCH, NH:2 * NH], bf, ALU.add)
            nc.vector.tensor_tensor(sm[:, 1, :], g.IF[:NS, NCH, 0:NH], bif[:NS, 0:NH], ALU.add)
            nc.vector.tensor_tensor(sm[:, 2, :], g.IF[:NS, NCH, NH:2 * NH], bif[:NS, NH:2 * NH], ALU.add).then_inc(biased, 1)
            split_lo(0, 1)
            nc.vector.tensor_scalar(hnw[:, :], hnw[:, :], 0.25, None, ALU.mult)
            link(nc.vector.tensor_scalar(cw[:, :, :], cw[:, :, :], 0.5, None, ALU.mult))
            dve.wait_ge(softplus, 1)
            nc.vector.scalar_tensor_tensor(out=tk["f_log"][:, :], in0=tk["f_log"][:, :], scalar=0.0, in1=tk["f_abs"][:, :],
                                           op0=ALU.min, op1=ALU.subtract).then_inc(lf_set, 1)
            link(nc.vector.scalar_tensor_tensor(out=sm[:, 8, :], in0=sm[:, 2, :], scalar=0.0, in1=sm[:, 9, :],
                                                op0=ALU.min, op1=ALU.subtract))
            link(nc.vector.tensor_tensor(sm[:, 5, :], sm[:, 8, :], sm[:, 0, :], ALU.add))
            link(nc.vector.tensor_tensor(sm[:, 3, :], sm[:, 5, :], sm[:, 1, :], ALU.max))
            link(nc.vector.tensor_tensor(sm[:, 5, :], sm[:, 5, :], sm[:, 3, :], ALU.subtract))
            link(nc.vector.tensor_tensor(sm[:, 6, :], sm[:, 1, :], sm[:, 3, :], ALU.subtract))
            dve.wait_ge(b_mm, 1)
            nc.vector.tensor_copy(tk["b_cum"][:, :], PS[:, 0, 0:HC])
            nc.vector.tensor_copy(rowA[0:1, 1, 0:HC], PS[0:1, 1, 0:HC])
            nc.vector.tensor_copy(cs[:, :, :], PN[0][:, 0:2 * NS * KB].rearrange("p (k n) -> p k n", k=KB))
            nc.vector.tensor_tensor(tk["a_in"][:, :], tk["a_in"][:, :], PS[:, 0, 0:HC], ALU.subtract).then_inc(a_set, 1)
            dve.wait_ge(a_mm, 1)
            link(nc.vector.tensor_copy(aT, PT[0][0:HC, 0, :]))
            nc.vector.tensor_tensor_scan(cM, aT, aT, -BIG, ALU.max, ALU.max).then_inc(cm_set, 1)
            dve.wait_ge(al_mm, 1)
            link(nc.vector.tensor_copy(rowA[0:1, 0, 0:HC], PS[0:1, 2, 0:HC]))
            for h in range(NH):
                last = nc.vector.tensor_tensor_scan(rowA[0:1, 2, NH + h:NH + HC:NH], rowA[0:1, 0, h:HC:NH],
                                                    rowA[0:1, 1, h:HC:NH], 0.0, ALU.max, ALU.add)
            link(last)
            nc.vector.tensor_tensor(rowA[0:1, 3, 0:HC], rowA[0:1, 2, 0:HC], rowA[0:1, 0, 0:HC], ALU.max).then_inc(m_set, 1)
            dve.wait_ge(m_mm, 1)
            nc.vector.tensor_copy(tk["m_prev"][:, :], PT[1][:, 0, 0:HC])
            nc.vector.tensor_tensor(tk["w_end"][:, :], tk["a_in"][:, :], PT[1][:, 1, 0:HC], ALU.subtract)
            link(nc.vector.tensor_copy(col[:, :], PT[1][0:HC, 2, 0:1]))
            nc.vector.tensor_tensor(tk["f_end"][:, :], tk["m_prev"][:, :], PT[1][:, 1, 0:HC], ALU.subtract)
            link(nc.vector.tensor_scalar(cM, cM, col[:, 0:1], None, ALU.max))
            nc.vector.tensor_scalar(aT, cM, -1.0, None, ALU.mult).then_inc(M_set, 1)
            dve.wait_ge(mt_mm, 1)
            nc.vector.tensor_tensor(tk["exp_negm"][:, :], tk["b_cum"][:, :], PT[0][:, 0, 0:HC], ALU.add).then_inc(exps_in, 1)

            split_lo(1, 0)
            with dve.Fori(1, NP1) as h:
                split_lo(F1 + h, 1)
                split_lo(F1 + h + 1, 0)
            dve.wait_ge(exps_set, 1)

            def silu_z(pair, par, t, zn):
                c0, n = TILES[t]
                b = (par * NTILE + t) % 2
                dve.wait_ge(z_set, zn)
                nc.vector.scalar_tensor_tensor(out=E1[:, c0:c0 + n], in0=ZT[:, b, 0:n], scalar=1.0, in1=G[b][:, 0:n],
                                               op0=ALU.add, op1=ALU.mult).then_inc(free[b], 1)

            with dve.Fori(0, NP2) as i:
                own.enter(i, 1)
                pair = F2 + i
                split_lo(pair, 1)
                split_lo(pair + 1, 0)
                dve.wait_ge(row_out[1], 1 + 16 * (row_gate + i))
                for t in range(NTILE):
                    silu_z(pair, 1, t, NTILE * i + t + 1)
                block_waits(dve, pair, 1)
                link(nc.vector.scalar_tensor_tensor(out=E1[:, 0:T], in0=E0[:, 0:T], scalar=1.0, in1=E1[:, 0:T],
                                                    op0=ALU.add, op1=ALU.mult))
                nc.vector.tensor_scalar(E1[:, 0:T], E1[:, 0:T], hnw[:, bass.ds(i, 1)], None, ALU.mult).then_inc(gate_set, 1)
            own.leave(NP2)
            nc.vector.memset(E0[:, 0:2], 0.0).then_inc(u_used, 1)

            def chunk_dve(c, s):
                if s == 0:
                    dve.wait_ge(kq_in, 48 * (c + 1))
                    dve.wait_ge(sq_set, 1 + NH * c)
                    nc.vector.tensor_tensor(Dm[:, :, :], nM[:, :, :], mask[:, :].unsqueeze(1).to_broadcast([P, NH, P]),
                                            ALU.min).then_inc(dpre, 1)
                    dve.wait_ge(kt_done, c + 1)
                    dve.wait_ge(cu_done, 1 + NH * c)
                    nc.vector.tensor_tensor(KW[:, :, :], PT[0][:, :, :], bc(tk["w_end"][:, bass.ds(NH * c, NH)], P),
                                            ALU.mult).then_inc(kw_set, 1)
                    dve.wait_ge(wint_set, c + 1)
                    nc.vector.tensor_tensor(QW[:, :, :], QW[:, :, :], qT[:, :, :], ALU.mult).then_inc(qw_set, 1)
                    dve.wait_ge(s_done, c + 1)
                    dve.wait_ge(dexp_set, c + 1)
                    dve.wait_ge(num_done, 1 + NH * c)
                    nc.vector.tensor_tensor(PT_[:, :, :], PS[:, :, :], Dm[:, :, :], ALU.mult).then_inc(p_set, 1)
                elif 2 <= s < 2 + NH:
                    h = s - 2
                    ch = bass.ds(NH * c + h, 1)
                    dve.wait_ge(num_done, 1 + NH * c + h + 1)
                    link(nc.vector.tensor_scalar(den[:, 0, 0:1], PN[h % 2][:, DHV:DHV + 1], -1.0, tk["exp_negm"][:, ch],
                                                 ALU.mult, ALU.max))
                    link(nc.vector.tensor_tensor(den[:, 0, 1:2], PN[h % 2][:, DHV:DHV + 1], den[:, 0, 0:1], ALU.max))
                    link(nc.vector.reciprocal(den[:, 1, 0:1], den[:, 0, 1:2]))
                    if h == 0:
                        dve.wait_ge(ht_done, 1 + c)
                    nc.vector.tensor_scalar(HB[:, h, :], PN[h % 2][:, 0:DHV], den[:, 1, 0:1], None, ALU.mult).then_inc(h_set, 1)
                    dve.wait_ge(cu_done, 1 + NH * c + h + 1)
                    nc.vector.scalar_tensor_tensor(out=CS[:, h, :], in0=CS[:, h, :], scalar=tk["f_end"][:, ch], in1=PC[:, 0:DHV + 1],
                                                   op0=ALU.mult, op1=ALU.add).then_inc(c_set, 1)
                elif s == 6:
                    dve.wait_ge(sq_set, 1 + NH * (c + 1))
                    nc.vector.tensor_scalar(ss[:, 1, :], ss[:, 0, :], 1.0 / DHV, EPS, ALU.mult, ALU.add).then_inc(var_set, 1)
                elif s == 7:
                    dve.wait_ge(rs_set, c + 1)
                    nc.vector.tensor_tensor(HB[:, :, :], HB[:, :, :], bc(ss[:, 2, :], DHV), ALU.mult).then_inc(hn_set, 1)
                elif s == 8:
                    dve.wait_ge(ht_done, 1 + c + 1)
                    dve.wait_ge(gate_in, 16 * (c + 1))
                    nc.vector.tensor_tensor(GT[:, 0:4, :], GT[:, 0:4, :], PT[0][:, :, :], ALU.mult)
                    nc.vector.tensor_tensor(GT[:, 4:8, :], GT[:, 4:8, :], PT[1][:, :, :], ALU.mult).then_inc(hg_set, 1)

            def conv_tile(i, t):
                c0, n = TILES[t]
                w = [cw[:, j, bass.ds(i, 1)] for j in range(CW)]
                m = min(n, L - c0)
                link(nc.vector.tensor_scalar(CV[:, 0:n], E0[:, 2 + c0:2 + c0 + n], w[2], None, ALU.mult))
                link(nc.vector.scalar_tensor_tensor(out=CV[:, 0:m], in0=E0[:, 1 + c0:1 + c0 + m], scalar=w[1], in1=CV[:, 0:m],
                                                    op0=ALU.mult, op1=ALU.add))
                if m < n:
                    st = cs[:, bass.ds(i, 1), :].rearrange("p a (b r) -> p (a b) r", r=2)
                    for r in range(2):
                        link(nc.vector.scalar_tensor_tensor(out=CV[:, m:n], in0=st[:, :, r], scalar=w[r], in1=CV[:, m:n],
                                                            op0=ALU.mult, op1=ALU.add))
                ins = nc.vector.scalar_tensor_tensor(out=CV[:, 0:m], in0=E0[:, c0:c0 + m], scalar=w[0], in1=CV[:, 0:m],
                                                     op0=ALU.mult, op1=ALU.add)
                return ins

            with dve.Fori(0, KB) as i:
                own.enter(i, 6 * NH + 4 * NTILE + 1)
                pair = F3 + 2 * i
                split_lo(pair, 1)
                for s in range(NTILE):
                    chunk_dve(2 * i, s)
                split_lo(pair + 1, 0)
                for s in range(NTILE):
                    chunk_dve(2 * i, NTILE + s)
                    if s == 0:
                        block_waits(dve, pair, 0)
                    c0, n = TILES[s]
                    b = (NTILE + s) % 2
                    dve.wait_ge(done, 1 + 2 * NTILE * pair + NTILE + s + 1)
                    nc.vector.tensor_tensor(E0[:, 2 + c0:2 + c0 + n], E0[:, 2 + c0:2 + c0 + n], G[b][:, 0:n], ALU.mult).then_inc(free[b], 1)
                split_lo(pair + 1, 1)
                dve.wait_ge(row_out[1], 1 + 16 * (row_conv + i))
                for s in range(NTILE):
                    chunk_dve(2 * i + 1, s)
                    silu_z(pair + 1, 0, s, NTILE * (NP2 + i) + s + 1)
                split_lo(pair + 2, 0)
                for s in range(NTILE):
                    chunk_dve(2 * i + 1, NTILE + s)
                    if s == 0:
                        block_waits(dve, pair, 1)
                        block_waits(dve, pair + 1, 0)
                    else:
                        dve.wait_ge(free[(NTILE + s - 1) % 2], NTILE * (pair + 1) + (NTILE + s - 1) // 2 + 2)
                    ins = conv_tile(i, s)
                    if s == NTILE - 1:
                        ins.then_inc(u_used, 1)
                        dve.wait_ge(u_used, i + 2)
                    else:
                        link(ins)
                    c0, n = TILES[s]
                    b = (NTILE + s) % 2
                    link(nc.vector.tensor_tensor(CV[:, 0:n], CV[:, 0:n], E1[:, c0:c0 + n], ALU.mult))
                    dve.wait_ge(done, 1 + 2 * NTILE * (pair + 1) + NTILE + s + 1)
                    nc.vector.tensor_tensor(E1[:, c0:c0 + n], CV[:, 0:n], G[b][:, 0:n], ALU.mult).then_inc(free[b], 1)
            own.leave(KB)

            dve.wait_ge(ct_mm, 1)
            HB8 = HB[:, :, :].rearrange("p h (a d) -> p (h a) d", a=2)
            nc.vector.tensor_copy(HB8[:, 0:4, :], PT[0][:, :, :])
            nc.vector.tensor_copy(HB8[:, 4:8, :], PT[1][:, :, :]).then_inc(ct_set, 1)
            split_lo(F4, 1)
            split_lo(F4 + 1, 0)
            dve.wait_ge(dec_mm, 1)
            nc.vector.tensor_copy(PT_[:NS, :, :], PS[:NS, :, :])
            nc.vector.tensor_copy(KW[:NS, :, :].rearrange("p h d -> p (h d)"), PN[0][:NS, :])
            vd = dec[:, 5, :]
            link(nc.vector.tensor_copy(vd.rearrange("p (b k) -> p k b", k=KB), PN[1][:, 0:KB * NS].rearrange("p (k b) -> p k b", k=KB)))
            link(nc.vector.tensor_tensor(Dm[:NS, :, :], KW[:NS, :, :], bc(sm[:, 6, :], P), ALU.mult))
            link(nc.vector.tensor_tensor(QW[:NS, :, :], QW[:NS, :, :], bc(sm[:, 5, :], P), ALU.mult))
            link(nc.vector.tensor_tensor(QW[:NS, :, :], QW[:NS, :, :], Dm[:NS, :, :], ALU.add))
            link(nc.vector.tensor_tensor(Dm[:NS, :, :], QW[:NS, :, :], PT_[:NS, :, :], ALU.mult))
            link(nc.vector.tensor_reduce(sm[:, 8, :], Dm[:NS, :, :], AX.X, ALU.add))
            link(nc.vector.scalar_tensor_tensor(out=sm[:, 9, :], in0=sm[:, 8, :], scalar=-1.0, in1=sm[:, 4, :],
                                                op0=ALU.mult, op1=ALU.max))
            link(nc.vector.tensor_tensor(sm[:, 9, :], sm[:, 9, :], sm[:, 8, :], ALU.max))
            nc.vector.reciprocal(sm[:, 7, :], sm[:, 9, :]).then_inc(dec_rows, 1)
            dve.wait_ge(dec_bc, 32)
            vd3 = vd.rearrange("p (n a) -> p n a", a=2)
            link(nc.vector.tensor_tensor(vd3, vd3, bc(dec[:, 0, NS * NH:2 * NS * NH], 2), ALU.mult))
            dve.wait_ge(c_out, 16 * 5)

            def decode(b):
                dve.wait_ge(dec_kq_in, 32 * (b + 1))
                dve.wait_ge(dec_c_in, 16 * (b + 1))
                GT4 = GT[:, :, :].rearrange("p (h a) d -> p h (a d)", a=2)
                link(nc.vector.tensor_tensor(GT4, GT4, bc(dec[:, 0, sl(b, NH)], 2 * P), ALU.mult))
                vb = dec[:, 5, sl(b, KB)].rearrange("p (h a) -> p h a", a=2)
                for a in range(2):
                    last = nc.vector.tensor_tensor(HB[:, :, a * P:(a + 1) * P], kT[:, :, :], bc(vb[:, :, a], P), ALU.mult)
                link(last)
                link(nc.vector.tensor_tensor(GT[:, :, :], GT[:, :, :], HB8, ALU.add))
                for a in range(2):
                    last = nc.vector.tensor_tensor(HB[:, :, a * P:(a + 1) * P], qT[:, :, :], GT4[:, :, a * P:(a + 1) * P], ALU.mult)
                link(last)
                nc.vector.tensor_reduce(dec[:, 2, sl(b, KB)], HB8, AX.X, ALU.add).then_inc(dec_upd, 1)

            with dve.Fori(0, NP4 - 2) as i:
                own.enter(i, 4)
                split_lo(F4 + i + 1, 1)
                decode(i)
                split_lo(F4 + i + 2, 0)
            own.leave(NP4 - 2)
            split_lo(NPAIR - 1, 1)
            decode(NS - 2)
            decode(NS - 1)
            dve.wait_ge(dec_upd, 1 + NS)
            num3 = dec[:, 2, :].rearrange("p (n a) -> p n a", a=2)
            link(nc.vector.tensor_tensor(num3, num3, bc(dec[:, 1, 0:NS * NH], 2), ALU.mult))
            nc.vector.tensor_tensor(dec[:, 3, :], dec[:, 2, :], dec[:, 2, :], ALU.mult).then_inc(dec_sq, 1)
            dve.wait_ge(dec_sum, 1)
            link(nc.vector.tensor_reduce(dec[:, 4, 0:NS * NH], PN[0][:, 0:2 * NS * NH].rearrange("p (n a) -> p n a", a=2), AX.X, ALU.add))
            nc.vector.tensor_scalar(dec[:, 3, 0:NS * NH], dec[:, 4, 0:NS * NH], 1.0 / DHV, EPS, ALU.mult, ALU.add).then_inc(dec_var, 1)
            dve.wait_ge(dec_rs, 1)
            link(nc.vector.tensor_tensor(num3, num3, bc(dec[:, 4, 0:NS * NH], 2), ALU.mult))
            nc.vector.tensor_tensor(dec[:, 6, :].rearrange("p (k b) -> p b k", k=KB), dec[:, 2, :].rearrange("p (b k) -> p b k", k=KB),
                                    dec[:, 7, :].rearrange("p (k b) -> p b k", k=KB), ALU.mult).then_inc(dec_h, 1)

        @block.tensor
        def _(pe):
            for s in from_one["pe"]:
                pe.sem_inc(s, 1)

            def tile(pair, par, t):
                c0, n = TILES[t]
                j = par * NTILE + t
                if t == 0:
                    pe.wait_ge(w_ready, 2 * pair + par + 1)
                pe.wait_ge(free[j % 2], NTILE * pair + j // 2 + 1)
                step = 0
                for k in range(KB):
                    for w, x in ((WH, g.RH), (WH, g.RL), (WL, g.RH)):
                        last = nc.tensor.matmul(G[j % 2][:, 0:n], w[:, par, k, :], x[:, k, c0:c0 + n],
                                                start=(step == 0), stop=(step == 3 * KB - 1))
                        step += 1
                last.then_inc(done, 1)

            def conv_state():
                pe.wait_ge(const_in, 144)
                for k in range(KB):
                    src = (csr if k < 4 else csr2)[:, (k % 4) * P:(k % 4 + 1) * P]
                    nc.tensor.transpose(PN[0][:, k * 2 * NS:(k + 1) * 2 * NS], src, g.ident[:2 * NS, :2 * NS])

            def cumulate():
                pe.wait_ge(const_set, 6)
                pe.wait_ge(lf_set, 1)
                nc.tensor.matmul(PS[:, 0, 0:HC], cumU[:, :], tk["f_log"][:, :], start=True, stop=True)
                nc.tensor.matmul(PS[0:1, 1, 0:HC], ones[:, 0:1], tk["f_log"][:, :], start=True, stop=True).then_inc(b_mm, 1)

            def turn_a():
                pe.wait_ge(a_set, 1)
                nc.tensor.transpose(PT[0][0:HC, 0, :], tk["a_in"][:, :], g.ident[:, :]).then_inc(a_mm, 1)

            def last_a():
                pe.wait_ge(cm_set, 1)
                nc.tensor.matmul(PS[0:1, 2, 0:HC], cM[:, P - 1:P], g.ident[0:HC, 0:HC], start=True, stop=True).then_inc(al_mm, 1)

            def spread_m():
                pe.wait_ge(m_set, 1)
                nc.tensor.matmul(PT[1][:, 0, 0:HC], ones[0:1, :], rowA[0:1, 2, 0:HC], start=True, stop=True)
                nc.tensor.matmul(PT[1][:, 1, 0:HC], ones[0:1, :], rowA[0:1, 3, 0:HC], start=True, stop=True)
                nc.tensor.matmul(PT[1][0:HC, 2, 0:1], rowA[0:1, 2, 0:HC], ones[0:1, 0:1], start=True, stop=True).then_inc(m_mm, 1)

            def turn_M():
                pe.wait_ge(M_set, 1)
                nc.tensor.transpose(PT[0][:, 0, 0:HC], cM, g.ident[0:HC, 0:HC]).then_inc(mt_mm, 1)

            steps = {2: conv_state, 3: cumulate, 4: turn_a, 5: last_a, 6: spread_m, 7: turn_M}
            for t in range(2 * NTILE):
                if t in steps:
                    steps[t]()
                tile(0, t // NTILE, t % NTILE)

            with pe.Fori(1, NP1 + NP2) as i:
                for par in range(2):
                    for t in range(NTILE):
                        tile(i, par, t)

            def chunk_pe(c, s):
                if s == 0:
                    pe.wait_ge(kq_in, 48 * (c + 1))
                    pe.wait_ge(p_set, 1 + c)
                    for h in range(NH):
                        last = nc.tensor.matmul(PS[:, h, :], kT[:, h, :], qT[:, h, :], start=True, stop=True)
                    last.then_inc(s_done, 1)
                    pe.wait_ge(hg_set, 1 + c)
                    for h in range(NH):
                        last = nc.tensor.transpose(PT[0][:, h, :], kT[:, h, :], g.ident[:, :])
                    last.then_inc(kt_done, 1)
                elif 2 <= s < 2 + NH:
                    h = s - 2
                    if h == 0:
                        pe.wait_ge(v_in, 16 * (c + 1))
                        pe.wait_ge(p_set, 1 + c + 1)
                        pe.wait_ge(qw_set, c + 1)
                        pe.wait_ge(kw_set, c + 1)
                    pe.wait_ge(h_set, NH * c + h + 1)
                    pe.wait_ge(c_set, NH * c + h + 1)
                    nc.tensor.matmul(PN[h % 2][:, 0:DHV + 1], PT_[:, h, :], va[:, h, :], start=True, stop=False)
                    nc.tensor.matmul(PN[h % 2][:, 0:DHV + 1], QW[:, h, :], CS[:, h, :], start=False, stop=True).then_inc(num_done, 1)
                    pe.wait_ge(c_set, NH * c + h + NH)
                    nc.tensor.matmul(PC[:, 0:DHV + 1], KW[:, h, :], va[:, h, :], start=True, stop=True).then_inc(cu_done, 1)
                elif s == 8:
                    pe.wait_ge(hn_set, c + 1)
                    for k in range(KB):
                        last = nc.tensor.transpose(PT[k // 4][:, k % 4, :], HB[:, k // 2, (k % 2) * P:(k % 2 + 1) * P], g.ident[:, :])
                    last.then_inc(ht_done, 1)

            with pe.Fori(0, KB) as i:
                for q in range(4):
                    for t in range(NTILE):
                        chunk_pe(2 * i + q // 2, (q % 2) * NTILE + t)
                        tile(F3 + 2 * i + q // 2, q % 2, t)

            pe.wait_ge(c_set, HC + NH)
            pe.wait_ge(hg_set, 1 + NCH)
            for k in range(KB):
                last = nc.tensor.transpose(PT[k // 4][:, k % 4, :], CS[:, k // 2, (k % 2) * P:(k % 2 + 1) * P], g.ident[:, :])
            last.then_inc(ct_mm, 1)

            for t in range(2 * NTILE):
                tile(F4, t // NTILE, t % NTILE)
            pe.wait_ge(dec_in, 80)
            for h in range(NH):
                nc.tensor.transpose(PS[0:NS, h, :], GT[:, 0, h * NS:(h + 1) * NS], g.ident[:, :])
                nc.tensor.transpose(PN[0][0:NS, h * P:(h + 1) * P], GT[:, 0, (NH + h) * NS:(NH + h + 1) * NS], g.ident[:, :])
            for k in range(KB):
                last = nc.tensor.transpose(PN[1][:, k * NS:(k + 1) * NS], va[0:NS, k // 2, (k % 2) * P:(k % 2 + 1) * P], g.ident[0:NS, 0:NS])
            last.then_inc(dec_mm, 1)
            with pe.Fori(1, NP4 - 1) as i:
                for t in range(2 * NTILE):
                    tile(F4 + i, t // NTILE, t % NTILE)
            for t in range(2 * NTILE):
                if t == NTILE + 2:
                    pe.wait_ge(dec_sq, 1)
                    nc.tensor.matmul(PN[0][:, 0:2 * NS * NH], ones[:, :], dec[:, 3, :], start=True, stop=True).then_inc(dec_sum, 1)
                tile(NPAIR - 1, t // NTILE, t % NTILE)

    ctx.close()


def phase_c(nc, g):
    ctx = ExitStack()
    sem = lambda n: ctx.enter_context(nc.semaphore("c_" + n))
    NO = KB
    NB = 8
    AH = [sbuf(nc, ctx, f"act_hi{j}", [P, KB, TN], F32R) for j in range(2)]
    AL = [sbuf(nc, ctx, f"act_lo{j}", [P, KB, TN], F32R) for j in range(2)]
    ST = [sbuf(nc, ctx, f"act_stage{j}", [P, KB, TN]) for j in range(2)]
    TG = [sbuf(nc, ctx, f"tanh_gate{j}", [P, KB, TN]) for j in range(2)]
    TMP = sbuf(nc, ctx, "c_part", [P, 2, TN])
    MX = sbuf(nc, ctx, "mix", [P, KB, TN])
    G = [psum(nc, ctx, f"c_g{j}", [P, 512]) for j in range(NB)]

    slots = [g.S[:, j, 0:D] for j in range(2)]
    for st in ST:
        flat = st[:, :, :].rearrange("p k n -> p (k n)")
        slots += [flat[:, 0:D], flat[:, D:2 * D]]
    w_in_s = g.stage_in["wc"] + [sem(f"w_in{j}") for j in range(2, 6)]
    PLACE = [0, 1, 0, 1, 2, 3, 0, 1, 2, 3, 4, 5, 2, 3, 4, 5] + [2, 3, 4, 5, 2, 3, 4, 5]
    NW = 2 * KB
    PARTS = [(0, 1), (1, 4), (4, KB)]

    w_hi, w_ready = sem("w_hi"), sem("w_ready")
    st_in = [sem("st_in0"), sem("st_in1")]
    st_first, part_hi, part_ready = sem("st_first"), sem("part_hi"), sem("part_ready")
    tg_in = [sem("tg_in0"), sem("tg_in1")]
    a_hi = [sem("a_hi0"), sem("a_hi1")]
    a_ready = [sem("a_ready0"), sem("a_ready1")]
    done, free = sem("tile_done"), sem("bank_free")
    mix_set, mix_out = sem("mix_set"), g.mix_out

    acts = [g.hg_d, g.cv_d]
    tanhs = [g.tm_d, g.tc_d]
    wts = [w[0].rearrange("(k p) n -> k p n", p=P) for w in (g.w_proj_m, g.w_proj_c, g.w_out)]

    def cols(t):
        return slice(t * TN, t * TN + TN) if isinstance(t, int) else bass.ds(t * TN, TN)

    def target(w, b):
        c0 = D if KB <= b < NW else 0
        return w[:, b % KB, c0:c0 + D]

    with nc.Block() as block:

        @block.sync
        def _(sp):
            def load_act(t, br):
                if isinstance(t, int) and t == 1:
                    sp.wait_ge(w_ready, NW - 2 + 2 * br)
                else:
                    sp.wait_ge(a_ready[br], t)
                sp.dma_start(ST[br][:, :, :], acts[br][:, :, cols(t)].rearrange("k p n -> p k n")).then_inc(st_in[br], 16)

            def load_tanh(t, br):
                if not (isinstance(t, int) and t == 0):
                    sp.wait_ge(free, 2 * NO * (t - 1) + NO * (br + 1) + NB)
                sp.dma_start(TG[br][:, :, :], tanhs[br][:, :, cols(t)].rearrange("k p n -> p k n")).then_inc(tg_in[br], 16)

            def load_w(b):
                place = PLACE[b]
                before = [a for a in range(b) if PLACE[a] == place and a // NW == b // NW]
                if before:
                    sp.wait_ge(w_ready, before[-1] + 1)
                elif place >= 2:
                    br = place // 2 - 1
                    sp.wait_ge(a_ready[br], NTC if b >= NW else 1)
                sp.dma_start(slots[place], wts[b // KB][b % KB]).then_inc(w_in_s[place], 16)

            first = acts[0][:, :, cols(0)].rearrange("k p n -> p k n")
            sp.dma_start(ST[0][:, 0:1, :], first[:, 0:1, :]).then_inc(st_first, 16)
            sp.dma_start(ST[0][:, 1:KB, :], first[:, 1:KB, :]).then_inc(st_in[0], 16)
            for b in range(2, 6):
                load_w(b)
            sp.dma_start(ST[1][:, :, :], acts[1][:, :, cols(0)].rearrange("k p n -> p k n")).then_inc(st_in[1], 16)
            load_w(6)
            load_w(7)
            load_tanh(0, 0)
            for b in range(8, NW - 2):
                load_w(b)
            load_tanh(0, 1)
            load_w(NW - 2)
            load_w(NW - 1)

            def body(t):
                load_act(t + 1, 0)
                load_act(t + 1, 1)
                load_tanh(t + 1, 0)
                sp.wait_ge(mix_set, t + 1)
                sp.dma_start(g.mix_d[:, :, cols(t)].rearrange("k p n -> p k n"), MX[:, :, :]).then_inc(mix_out, 16)
                load_tanh(t + 1, 1)

            body(0)
            with sp.Fori(1, NTC - 1) as t:
                body(t)
            sp.wait_ge(mix_out, 16 * (NTC - 1))
            for j in range(2):
                sp.dma_start(g.S[:, j, 0:D].rearrange("p (k n) -> p k n", k=KB),
                             g.mix_d[:, :, j * P:(j + 1) * P].rearrange("k p n -> p k n")).then_inc(g.stage_in["mix"][j], 16)
            for b in range(NW, NW + KB):
                load_w(b)
            sp.wait_ge(mix_set, NTC)
            sp.dma_start(g.mix_d[:, :, cols(NTC - 1)].rearrange("k p n -> p k n"), MX[:, :, :]).then_inc(mix_out, 16)

        @block.scalar
        def _(act):
            def split_hi(t, br):
                act.wait_ge(st_in[br], 16 * (t + 1))
                if not (isinstance(t, int) and t == 0):
                    act.wait_ge(done, 2 * NO * (t - 1) + NO * (br + 1))
                nc.scalar.activation(AH[br][:, :, :], ST[br][:, :, :], ACT.Copy).then_inc(a_hi[br], 1)

            def weights(b):
                place = PLACE[b]
                act.wait_ge(w_in_s[place], 16 * PLACE[:b + 1].count(place))
                if b >= NW:
                    act.wait_ge(done, 2 * NO * (NTC - 1) + NO)
                nc.scalar.activation(target(g.RH, b), slots[place], ACT.Copy).then_inc(w_hi, 1)

            weights(0)
            weights(1)
            for j, (k0, k1) in enumerate(PARTS):
                act.wait_ge(st_in[0] if j else st_first, 16)
                nc.scalar.activation(AH[0][:, k0:k1, :], ST[0][:, k0:k1, :], ACT.Copy).then_inc(part_hi, 1)
            for b in range(2, 6):
                weights(b)
            split_hi(0, 1)
            for b in range(6, NW):
                weights(b)
            with act.Fori(1, NTC) as t:
                split_hi(t, 0)
                split_hi(t, 1)
            for b in range(NW, NW + KB):
                weights(b)

        @block.vector
        def _(dve):
            def split_lo(t, br):
                dve.wait_ge(a_hi[br], t + 1 if br else t)
                nc.vector.tensor_tensor(AL[br][:, :, :], ST[br][:, :, :], AH[br][:, :, :].bitcast(F32),
                                        ALU.subtract).then_inc(a_ready[br], 1)

            def weights(b):
                dve.wait_ge(w_hi, b + 1)
                nc.vector.tensor_tensor(target(g.RL, b), slots[PLACE[b]], target(g.RHf, b), ALU.subtract).then_inc(w_ready, 1)

            def gate_m(t, o):
                dve.wait_ge(done, 2 * NO * t + o + 1)
                nc.vector.scalar_tensor_tensor(out=MX[:, o, :], in0=TG[0][:, o, :], scalar=1.0, in1=G[o % NB][:, 0:TN],
                                               op0=ALU.add, op1=ALU.mult).then_inc(free, 1)

            def gate_c(t, o):
                dve.wait_ge(done, 2 * NO * t + NO + o + 1)
                nc.vector.scalar_tensor_tensor(out=TMP[:, o % 2, :], in0=TG[1][:, o, :], scalar=1.0, in1=G[o % NB][:, 0:TN],
                                               op0=ALU.add, op1=ALU.mult).then_inc(free, 1)
                dve.wait_ge(free, 2 * NO * t + NO + o + 1 + NB)
                return nc.vector.tensor_tensor(MX[:, o, :], MX[:, o, :], TMP[:, o % 2, :], ALU.add)

            nc.vector.memset(TMP[:, :, :], 0.0).then_inc(free, NB)
            weights(0)
            for j, (k0, k1) in enumerate(PARTS):
                dve.wait_ge(part_hi, j + 1)
                last = nc.vector.tensor_tensor(AL[0][:, k0:k1, :], ST[0][:, k0:k1, :], AH[0][:, k0:k1, :].bitcast(F32),
                                               ALU.subtract).then_inc(part_ready, 1)
                if j == 0:
                    weights(1)
            dve.wait_ge(part_ready, len(PARTS))
            dve.sem_inc(a_ready[0], 1)
            for b in range(2, 6):
                weights(b)
            split_lo(0, 1)
            for b in range(6, KB + 1):
                weights(b)
            dve.wait_ge(tg_in[0], 16)
            for o in range(NO):
                gate_m(0, o)
                if o % 3 == 2:
                    weights(KB + 1 + o // 3)
            for b in range(KB + 3, NW):
                weights(b)
            split_lo(1, 0)
            dve.wait_ge(tg_in[1], 16)
            for o in range(NO):
                ins = gate_c(0, o)
            ins.then_inc(mix_set, 1)
            split_lo(1, 1)

            def body(t, last=False):
                dve.wait_ge(tg_in[0], 16 * (t + 1))
                dve.wait_ge(mix_out, 16 * t)
                for o in range(NO):
                    gate_m(t, o)
                if not last:
                    split_lo(t + 1, 0)
                dve.wait_ge(tg_in[1], 16 * (t + 1))
                for o in range(NO):
                    if last:
                        weights(NW + o)
                    ins = gate_c(t, o)
                ins.then_inc(mix_set, 1)
                if not last:
                    split_lo(t + 1, 1)

            with dve.Fori(1, NTC - 1) as t:
                body(t)
            body(NTC - 1, True)

        @block.tensor
        def _(pe):
            def product(br, o, k):
                c0 = br * D + o * P
                for m, (w, x) in enumerate(((g.RH, AH[br]), (g.RH, AL[br]), (g.RL, AH[br]))):
                    last = nc.tensor.matmul(G[o % NB][:, 0:TN], w[:, k, c0:c0 + P], x[:, k, :],
                                            start=(k == 0 and m == 0), stop=(k == KB - 1 and m == 2))
                if k == KB - 1:
                    last.then_inc(done, 1)

            for br in range(2):
                for k in range(KB):
                    pe.wait_ge(w_ready, br * KB + k + 1)
                    for j, (k0, _) in enumerate(PARTS):
                        if br == 0 and k == k0:
                            pe.wait_ge(part_ready, j + 1)
                    if br == 1 and k == 0:
                        pe.wait_ge(a_ready[1], 1)
                    for o in range(NO):
                        if k == 0:
                            pe.wait_ge(free, br * NO + o + 1)
                        product(br, o, k)
            with pe.Fori(1, NTC) as t:
                for br in range(2):
                    pe.wait_ge(a_ready[br], t + 1)
                    for o in range(NO):
                        pe.wait_ge(free, 2 * NO * t + br * NO + o + 1)
                        for k in range(KB):
                            product(br, o, k)

    ctx.close()


def phase_d(nc, g):
    ctx = ExitStack()
    sem = lambda n: ctx.enter_context(nc.semaphore("d_" + n))
    N = D // 2
    WH, WL = g.RH[:, :, 0:D], g.RL[:, :, 0:D]
    MS = [g.S[:, j, 0:D].rearrange("p (k n) -> p k n", k=KB) for j in range(2)]
    MH = [sbuf(nc, ctx, f"mix_hi{j}", [P, KB, P], F32R) for j in range(2)]
    ML = [sbuf(nc, ctx, f"mix_lo{j}", [P, KB, P], F32R) for j in range(2)]
    X = [sbuf(nc, ctx, f"x_res{j}", [P, D]) for j in range(2)]
    Y = [sbuf(nc, ctx, f"y{j}", [P, D]) for j in range(2)]
    junk = sbuf(nc, ctx, "d_junk", [P, D])
    fw = sbuf(nc, ctx, "final_w", [P, D])
    stat = sbuf(nc, ctx, "d_stat", [P, 3, 2])
    half = sbuf(nc, ctx, "d_half", [P, 1])
    G = [psum(nc, ctx, f"d_g{j}", [P, N]) for j in range(4)]

    m_in = g.stage_in["mix"]
    x_in = [sem("x_in0"), sem("x_in1")]
    const_in, const_set = sem("const_in"), sem("const_set")
    m_hi, m_ready, done = sem("m_hi"), sem("m_ready"), sem("tile_done")
    summed, squared, var_set, rstd_set, y_set = sem("summed"), sem("squared"), sem("var_set"), sem("rstd_set"), sem("y_set")
    y_out = [sem("y_out0"), sem("y_out1")]

    xp = g.x_prompt[0].rearrange("(t p) d -> t p d", p=P)
    yp = g.y_prompt[0].rearrange("(t p) d -> t p d", p=P)

    def rows(i):
        return NS if isinstance(i, int) and i == NT - 1 else P

    def at(i):
        return slice(i * P, i * P + rows(i)) if isinstance(i, int) else bass.ds(i * P, P)

    def over_tiles(eng, body):
        with eng.Fori(0, NT // 2) as j:
            body(2 * j, 0)
            body(2 * j + 1, 1)
        body(NT - 1, 0)

    def slot_count(i, par):
        return i + 2 - par

    with nc.Block() as block:

        @block.sync
        def _(sp):
            def load_x(i, par):
                n = rows(i)
                if not isinstance(i, int) or i >= 2:
                    sp.wait_ge(summed, i - 1)
                src = g.x_sample[:, 0, :] if n == NS else (xp[i] if isinstance(i, int) else xp[bass.ds(i, 1)].rearrange("a p d -> (a p) d"))
                sp.dma_start(X[par][:n, :], src).then_inc(x_in[par], 16)

            def load(i, par):
                n = rows(i)
                sp.wait_ge(m_ready, i - 1)
                sp.dma_start(MS[par][:, :, 0:n], g.mix_d[:, :, at(i)].rearrange("k p n -> p k n")).then_inc(m_in[par], 16)
                load_x(i, par)

            def store(i, par):
                n = rows(i)
                sp.wait_ge(y_set, i + 1)
                dst = g.y_sample[:, 0, :] if n == NS else (yp[i] if isinstance(i, int) else yp[bass.ds(i, 1)].rearrange("a p d -> (a p) d"))
                sp.dma_start(dst, Y[par][:n, :]).then_inc(y_out[par], 16)

            load_x(0, 0)
            sp.dma_start(fw[:, :], g.final_norm_w.partition_broadcast(P)).then_inc(const_in, 16)
            load_x(1, 1)
            sp.wait_ge(g.mix_out, 16 * NTC)
            with sp.Fori(0, NT // 2 - 1) as j:
                for par in range(2):
                    load(2 * j + par + 2, par)
                    store(2 * j + par, par)
            load(NT - 1, 0)
            store(NT - 3, 0)
            store(NT - 2, 1)
            store(NT - 1, 0)
            sp.wait_ge(y_out[0], 16 * (NT // 2 + 1))
            sp.wait_ge(y_out[1], 16 * (NT // 2))

        @block.gpsimd
        def _(pool):
            nc.gpsimd.memset(half[:, :], -0.5).then_inc(const_set, 1)
            pool.wait_ge(const_set, 1)

            def rstd(i, par):
                n = rows(i)
                pool.wait_ge(var_set, i + 1)
                nc.gpsimd.tensor_tensor(stat[:n, 2, par:par + 1], stat[:n, 1, par:par + 1], half[:n, :], ALU.pow).then_inc(rstd_set, 1)

            over_tiles(pool, rstd)

        def hi(act, i, par):
            n = rows(i)
            act.wait_ge(m_in[par], 8 * slot_count(i, par))
            if not isinstance(i, int) or i >= 2:
                act.wait_ge(done, i - 1)
            nc.scalar.activation(MH[par][:, :, 0:n], MS[par][:, :, 0:n], ACT.Copy).then_inc(m_hi, 1)

        def lo(dve, i, par):
            n = rows(i)
            dve.wait_ge(m_hi, i + 1)
            nc.vector.tensor_tensor(ML[par][:, :, 0:n], MS[par][:, :, 0:n], MH[par][:, :, 0:n].bitcast(F32),
                                    ALU.subtract).then_inc(m_ready, 1)

        def with_lookahead(eng, ahead, finish):
            with eng.Fori(0, NT // 2 - 1) as j:
                for par in range(2):
                    ahead(eng, 2 * j + par + 1, 1 - par)
                    finish(2 * j + par, par)
            for i in range(NT - 3, NT):
                if i + 1 < NT:
                    ahead(eng, i + 1, (i + 1) % 2)
                finish(i, i % 2)

        @block.scalar
        def _(act):
            def square(i, par):
                n = rows(i)
                act.wait_ge(summed, i + 1)
                nc.scalar.activation(junk[:n, :], Y[par][:n, :], ACT.Square, accum_out=stat[:n, 0, par:par + 1]).then_inc(squared, 1)

            hi(act, 0, 0)
            with_lookahead(act, hi, square)

        @block.vector
        def _(dve):

            def finish(i, par):
                n = rows(i)
                dve.wait_ge(x_in[par], 8 * slot_count(i, par))
                dve.wait_ge(done, i + 1)
                if not isinstance(i, int) or i >= 2:
                    dve.wait_ge(y_out[par], 8 * (slot_count(i, par) - 2))
                for j in range(2):
                    last = nc.vector.scalar_tensor_tensor(out=Y[par][:n, j * N:(j + 1) * N], in0=G[2 * par + j][:n, :], scalar=0.5,
                                                          in1=X[par][:n, j * N:(j + 1) * N], op0=ALU.mult, op1=ALU.add)
                last.then_inc(summed, 1)
                dve.wait_ge(squared, i + 1)
                nc.vector.tensor_scalar(stat[:n, 1, par:par + 1], stat[:n, 0, par:par + 1], 1.0 / D, EPS, ALU.mult, ALU.add).then_inc(var_set, 1)
                dve.wait_ge(rstd_set, i + 1)
                nc.vector.scalar_tensor_tensor(out=Y[par][:n, :], in0=Y[par][:n, :], scalar=stat[:n, 2, par:par + 1], in1=fw[:n, :],
                                               op0=ALU.mult, op1=ALU.mult).then_inc(y_set, 1)

            lo(dve, 0, 0)
            dve.wait_ge(const_in, 16)
            with_lookahead(dve, lo, finish)

        @block.tensor
        def _(pe):
            def tile(i, par):
                n = rows(i)
                pe.wait_ge(m_ready, i + 1)
                if not isinstance(i, int) or i >= 2:
                    pe.wait_ge(summed, i - 1)
                for j in range(2):
                    step = 0
                    for k in range(KB):
                        for x, w in ((MH, WH), (MH, WL), (ML, WH)):
                            last = nc.tensor.matmul(G[2 * par + j][:n, :], x[par][:, k, 0:n], w[:, k, j * N:(j + 1) * N],
                                                    start=(step == 0), stop=(step == 3 * KB - 1))
                            step += 1
                last.then_inc(done, 1)

            tile(0, 0)
            tile(1, 1)
            with pe.Fori(1, NT // 2) as j:
                tile(2 * j, 0)
                tile(2 * j + 1, 1)
            tile(NT - 1, 0)

    ctx.close()


INPUTS = ["x_prompt", "x_sample", "state_mlstm_C", "state_mlstm_n", "state_mlstm_m", "state_conv", "norm_w", "w_in",
          "b_i", "b_f", "head_norm_w", "conv_w", "w_proj_m", "w_proj_c", "w_out", "final_norm_w"]
OUTPUTS = [("y_prompt", (1, L, D)), ("y_sample", (NS, 1, D)),
           ("new_C_prompt", (1, 1, NH, DHV, DQK)), ("new_n_prompt", (1, 1, NH, DQK)),
           ("new_m_prompt", (1, 1, NH)), ("new_conv_prompt", (1, 1, CW - 1, D)),
           ("new_C_sample", (1, NS, NH, DHV, DQK)), ("new_n_sample", (1, NS, NH, DQK)),
           ("new_m_sample", (1, NS, NH)), ("new_conv_sample", (1, NS, CW - 1, D))]


def kernel(**inputs):
    import concourse.bacc as bacc
    from concourse.bass_utils import run_bass_kernel_spmd

    nc = bacc.Bacc("TRN2", target_bir_lowering=False, num_devices=1, dynamic_dma_scratch_size=1024)
    arrays = {name: np.ascontiguousarray(inputs[name]) for name in INPUTS}
    ins = [nc.dram_tensor(name, a.shape, mybir.dt.from_np(a.dtype), kind="ExternalInput").ap() for name, a in arrays.items()]
    outs = [nc.dram_tensor(name, shape, F32, kind="ExternalOutput").ap() for name, shape in OUTPUTS]
    build(nc, ins, outs)
    results = run_bass_kernel_spmd(nc, [arrays], core_ids=[0]).results[0]
    return tuple(results[name] for name, _ in OUTPUTS)
```
